# Optimizing a Trainium2 kernel written in Bass

```python
import math
import jax, jax.numpy as jnp
from jax import lax
import numpy as np

D_MODEL = 1024
BATCH = 1
SEQ = 128
DEPTH = 2
DEC_BATCH = 1
DEC_SEQ = 512
PAST_LEN = 128

GRID_W = 64
N_EVEN = (DEPTH + 1) // 2
N_ODD = DEPTH // 2
N_MOD = 9
D_FF = 2816
H_A = 8
NOPE_A = 64
ROPE_A = 32
V_A = 64
Q_LORA = 384
KV_LORA = 256
H_B = 4
DH_B = 64
DV_B = 2 * DH_B
H_C = 4
DK_C = 64
DV_C = 128
GATE_RANK = 16
GATE_TAU = 16.0
H_D = 4
DK_D = 64
DV_D = 128
CHUNK = 64
Q_BLOCK = 128
ROPE_BASE = 10000.0
EPS = 1e-6

EVEN_SIZES = (Q_LORA, KV_LORA, ROPE_A, H_B * 2 * DH_B, H_B * 2 * DH_B, H_B * DV_B)
EVEN_CUTS = [sum(EVEN_SIZES[:i + 1]) for i in range(len(EVEN_SIZES) - 1)]
IN_EVEN = sum(EVEN_SIZES)
ODD_SIZES = (H_C * DK_C, H_C * DK_C, H_C * DV_C, 2 * GATE_RANK, H_C * DV_C,
             H_D * DK_D, H_D * DK_D, H_D * DV_D, H_D * DV_D)
ODD_CUTS = [sum(ODD_SIZES[:i + 1]) for i in range(len(ODD_SIZES) - 1)]
IN_ODD = sum(ODD_SIZES)
MIX_EVEN = H_A * V_A + H_B * DV_B
MIX_ODD = H_C * DV_C + H_D * DV_D

kernel_name = "hybrid_diffusion_prefix_step"

F32 = jnp.float32

def rmsnorm(x, g):
    xf = x.astype(F32)
    y = xf * lax.rsqrt(jnp.mean(xf * xf, axis=-1, keepdims=True) + EPS)
    return (y * g.astype(F32)).astype(x.dtype)

def group_norm(x, g):
    xf = x.astype(F32)
    mu = jnp.mean(xf, axis=-1, keepdims=True)
    var = jnp.mean(jnp.square(xf - mu), axis=-1, keepdims=True)
    return ((xf - mu) * lax.rsqrt(var + EPS) * g.astype(F32)).astype(x.dtype)

def rope_1d(x, pos):
    n = x.shape[-1]
    half = n // 2
    inv = ROPE_BASE ** (-jnp.arange(half, dtype=F32) * 2.0 / n)
    ang = pos[:, None] * inv[None, :]
    shp = (1, pos.shape[0]) + (1,) * (x.ndim - 3) + (half,)
    cos = jnp.cos(ang).reshape(shp)
    sin = jnp.sin(ang).reshape(shp)
    xf = x.astype(F32)
    x1, x2 = xf[..., :half], xf[..., half:]
    return jnp.concatenate([x1 * cos - x2 * sin, x2 * cos + x1 * sin], axis=-1).astype(x.dtype)

def rope_2d(x, row, col):
    n = x.shape[-1]
    return jnp.concatenate([rope_1d(x[..., :n // 2], row), rope_1d(x[..., n // 2:], col)], axis=-1)

def adaln(cond, w, b):
    m = jax.nn.silu(cond) @ w + b
    return m.reshape(cond.shape[0], 1, N_MOD, D_MODEL)

def modulate(x, g, shift, scale):
    return rmsnorm(x, g) * (1.0 + scale) + shift

def swiglu(x, wg, wu, wd):
    return (jax.nn.silu(x @ wg) * (x @ wu)) @ wd

def ffn_half(x, m, j, g, wg, wu, wd):
    return x + 0.5 * m[:, :, j + 2] * swiglu(modulate(x, g, m[:, :, j], m[:, :, j + 1]), wg, wu, wd)

def sweep_queries(fn, qs):
    b, t = qs[0].shape[:2]
    nb = t // Q_BLOCK
    blocks = tuple(jnp.moveaxis(q.reshape((b, nb, Q_BLOCK) + q.shape[2:]), 1, 0) for q in qs)
    out = lax.map(lambda qb: fn(*qb), blocks)
    return jnp.moveaxis(out, 0, 1).reshape((b, t) + out.shape[3:])

def mla_attend(q_nope, q_rope, k_nope, k_rope, v):
    scale = (NOPE_A + ROPE_A) ** -0.5

    def blk(qn, qr):
        s = (jnp.einsum('bqhd,bkhd->bhqk', qn, k_nope)
             + jnp.einsum('bqhr,bkr->bhqk', qr, k_rope)).astype(F32) * scale
        p = jax.nn.softmax(s, axis=-1).astype(v.dtype)
        return jnp.einsum('bhqk,bkhd->bqhd', p, v)

    return sweep_queries(blk, (q_nope, q_rope))

def diff_attend(q1, q2, k1, k2, v, lam):
    scale = DH_B ** -0.5

    def blk(q1b, q2b):
        s1 = jnp.einsum('bqhd,bkhd->bhqk', q1b, k1).astype(F32) * scale
        s2 = jnp.einsum('bqhd,bkhd->bhqk', q2b, k2).astype(F32) * scale
        p = jax.nn.softmax(s1, axis=-1) - lam * jax.nn.softmax(s2, axis=-1)
        return jnp.einsum('bhqk,bkhd->bqhd', p.astype(v.dtype), v)

    return sweep_queries(blk, (q1, q2))

def chunk_scan(q, k, v, g, s0):
    b, t, h, _ = q.shape
    nc = t // CHUNK
    g = g.astype(q.dtype)

    def to_chunks(a):
        return jnp.moveaxis(a.reshape((b, nc, CHUNK) + a.shape[2:]), 1, 0)

    mask = jnp.tril(jnp.ones((CHUNK, CHUNK), dtype=bool))[None, :, :, None, None]

    def step(s, inp):
        qc, kc, vc, gc = inp
        bc = jnp.cumsum(gc, axis=1)
        diff = bc[:, :, None] - bc[:, None]
        dec = jnp.exp(jnp.where(mask, diff, -jnp.inf))
        a = jnp.sum(qc[:, :, None] * kc[:, None] * dec, axis=-1)
        o = (jnp.einsum('btsh,bshv->bthv', a, vc)
             + jnp.einsum('bthk,bhkv->bthv', qc * jnp.exp(bc), s))
        blast = bc[:, -1]
        s_new = (jnp.exp(blast)[..., None] * s
                 + jnp.einsum('bshk,bshv->bhkv', kc * jnp.exp(blast[:, None] - bc), vc))
        return s_new.astype(s.dtype), o

    s_fin, o = lax.scan(step, s0, (to_chunks(q), to_chunks(k), to_chunks(v), to_chunks(g)))
    return jnp.moveaxis(o, 0, 1).reshape(b, t, h, v.shape[-1]), s_fin

def bidir_scan(q, k, v, g, s):
    o_f, s_f = chunk_scan(q, k, v, g[:, :, 0], s[:, 0])
    flip = lambda a: jnp.flip(a, axis=1)
    o_b, s_b = chunk_scan(flip(q), flip(k), flip(v), flip(g[:, :, 1]), s[:, 1])
    return o_f + flip(o_b), jnp.stack([s_f, s_b], axis=1)

def even_project(h, w_in, q_norm, w_uq, kv_norm):
    b, t, _ = h.shape
    cq, ckv, krope, qd, kd, vd = jnp.split(h @ w_in, EVEN_CUTS, axis=-1)
    q = (rmsnorm(cq, q_norm) @ w_uq).reshape(b, t, H_A, NOPE_A + ROPE_A)
    return (q[..., :NOPE_A], q[..., NOPE_A:], rmsnorm(ckv, kv_norm), krope,
            qd.reshape(b, t, H_B, 2 * DH_B), kd.reshape(b, t, H_B, 2 * DH_B), vd.reshape(b, t, H_B, DV_B))

def even_mix(q_nope, q_rope, ckv, krope, qd, kd, vd, w_ukv, lam_p, subln, w_out, lam_init):
    b, tk = ckv.shape[:2]
    bq, tq = q_nope.shape[:2]
    kv = (ckv @ w_ukv).reshape(b, tk, H_A, NOPE_A + V_A)
    o_a = mla_attend(q_nope, q_rope, kv[..., :NOPE_A], krope, kv[..., NOPE_A:])
    lp = lam_p.astype(F32)
    lam = jnp.exp(jnp.sum(lp[0] * lp[1])) - jnp.exp(jnp.sum(lp[2] * lp[3])) + lam_init
    o_b = diff_attend(qd[..., :DH_B], qd[..., DH_B:], kd[..., :DH_B], kd[..., DH_B:], vd, lam)
    o_b = rmsnorm(o_b, subln) * (1.0 - lam_init)
    o = jnp.concatenate([o_a.reshape(bq, tq, H_A * V_A), o_b.reshape(bq, tq, H_B * DV_B)], axis=-1)
    return o @ w_out

def odd_project(h, w_in, w_gate, b_gate, ret_decay):
    b, t, _ = h.shape
    gq, gk, gv, glr, gr, rq, rk, rv, rr = jnp.split(h @ w_in, ODD_CUTS, axis=-1)
    logit = jnp.einsum('btdr,drk->btdk', glr.reshape(b, t, 2, GATE_RANK), w_gate) + b_gate
    g_gla = (jax.nn.log_sigmoid(logit) / GATE_TAU).reshape(b, t, 2, H_C, DK_C)
    log_gamma = jnp.log1p(-jnp.exp2(-ret_decay)).astype(h.dtype)
    g_ret = jnp.broadcast_to(log_gamma[None, None, :, :, None], (b, t, 2, H_D, 1))
    gla = (gq.reshape(b, t, H_C, DK_C) * DK_C ** -0.5, gk.reshape(b, t, H_C, DK_C),
           gv.reshape(b, t, H_C, DV_C), g_gla, gr)
    ret = (rq.reshape(b, t, H_D, DK_D), rk.reshape(b, t, H_D, DK_D) * DK_D ** -0.5,
           rv.reshape(b, t, H_D, DV_D), g_ret, rr)
    return gla, ret

def odd_mix(gla, ret, s_gla, s_ret, gla_norm, ret_norm, w_out):
    gq, gk, gv, g_gla, gr = gla
    rq, rk, rv, g_ret, rr = ret
    b, t = gq.shape[:2]
    o_c, s_gla_new = bidir_scan(gq, gk, gv, g_gla, s_gla)
    o_d, s_ret_new = bidir_scan(rq, rk, rv, g_ret, s_ret)
    o_c = rmsnorm(o_c, gla_norm).reshape(b, t, H_C * DV_C) * jax.nn.silu(gr)
    o_d = group_norm(o_d, ret_norm).reshape(b, t, H_D * DV_D) * jax.nn.silu(rr)
    return jnp.concatenate([o_c, o_d], axis=-1) @ w_out, s_gla_new, s_ret_new

def setup_inputs(seed: int = 0) -> dict:
    key = jax.random.key(seed)
    ks = iter(jax.random.split(key, 40))

    def nrm(shape, scale=1.0):
        return jax.random.normal(next(ks), shape, dtype=F32) * scale

    def gain(shape):
        return 1.0 + nrm(shape, 0.02)

    return {
        "x_prompt": nrm((BATCH, SEQ, D_MODEL)),
        "x_sample": nrm((DEC_BATCH, DEC_SEQ, D_MODEL)),
        "cache_mla_ckv": nrm((DEC_BATCH, N_EVEN, PAST_LEN, KV_LORA)),
        "cache_mla_krope": nrm((DEC_BATCH, N_EVEN, PAST_LEN, ROPE_A)),
        "cache_diff_k": nrm((DEC_BATCH, N_EVEN, PAST_LEN, H_B, 2 * DH_B)),
        "cache_diff_v": nrm((DEC_BATCH, N_EVEN, PAST_LEN, H_B, DV_B)),
        "state_gla": nrm((DEC_BATCH, N_ODD, 2, H_C, DK_C, DV_C)),
        "state_ret": nrm((DEC_BATCH, N_ODD, 2, H_D, DK_D, DV_D)),
        "c": nrm((DEC_BATCH, D_MODEL)),
        "c_ctx": nrm((D_MODEL,)),
        "mod_w": nrm((DEPTH, D_MODEL, N_MOD * D_MODEL), D_MODEL ** -0.5),
        "mod_b": nrm((DEPTH, N_MOD * D_MODEL), 0.02),
        "norm_g": gain((DEPTH, 3, D_MODEL)),
        "ffn_w_gate": nrm((DEPTH, 2, D_MODEL, D_FF), D_MODEL ** -0.5),
        "ffn_w_up": nrm((DEPTH, 2, D_MODEL, D_FF), D_MODEL ** -0.5),
        "ffn_w_down": nrm((DEPTH, 2, D_FF, D_MODEL), D_FF ** -0.5),
        "even_w_in": nrm((N_EVEN, D_MODEL, IN_EVEN), D_MODEL ** -0.5),
        "mla_q_norm": gain((N_EVEN, Q_LORA)),
        "mla_w_uq": nrm((N_EVEN, Q_LORA, H_A * (NOPE_A + ROPE_A)), Q_LORA ** -0.5),
        "mla_kv_norm": gain((N_EVEN, KV_LORA)),
        "mla_w_ukv": nrm((N_EVEN, KV_LORA, H_A * (NOPE_A + V_A)), KV_LORA ** -0.5),
        "diff_lambda": nrm((N_EVEN, 4, DH_B), 0.1),
        "diff_subln": gain((N_EVEN, DV_B)),
        "even_w_out": nrm((N_EVEN, MIX_EVEN, D_MODEL), MIX_EVEN ** -0.5),
        "odd_w_in": nrm((N_ODD, D_MODEL, IN_ODD), D_MODEL ** -0.5),
        "gla_w_gate": nrm((N_ODD, 2, GATE_RANK, H_C * DK_C), GATE_RANK ** -0.5),
        "gla_b_gate": nrm((N_ODD, 2, H_C * DK_C), 0.1),
        "gla_norm": gain((N_ODD, DV_C)),
        "ret_decay": 5.0 + jnp.arange(H_D, dtype=F32)[None, None, :] + nrm((N_ODD, 2, H_D), 0.1),
        "ret_norm": gain((N_ODD, DV_D)),
        "odd_w_out": nrm((N_ODD, MIX_ODD, D_MODEL), MIX_ODD ** -0.5),
        "final_g": gain((D_MODEL,)),
    }

def reference(x_prompt, x_sample, cache_mla_ckv, cache_mla_krope, cache_diff_k, cache_diff_v,
              state_gla, state_ret, c, c_ctx, mod_w, mod_b, norm_g, ffn_w_gate, ffn_w_up, ffn_w_down,
              even_w_in, mla_q_norm, mla_w_uq, mla_kv_norm, mla_w_ukv, diff_lambda, diff_subln, even_w_out,
              odd_w_in, gla_w_gate, gla_b_gate, gla_norm, ret_decay, ret_norm, odd_w_out, final_g):
    b_p, t_p, _ = x_prompt.shape
    b_s, t_s, _ = x_sample.shape
    rows = t_s // GRID_W
    row = jnp.repeat(jnp.arange(rows), GRID_W).astype(F32)
    col = jnp.tile(jnp.arange(GRID_W), rows).astype(F32)
    tpos = jnp.arange(t_s, dtype=F32)

    xp, xs = x_prompt, x_sample
    new_ckv, new_krope, new_dk, new_dv, new_sg, new_sr = [], [], [], [], [], []
    for l in range(DEPTH):
        mp = adaln(c_ctx[None].astype(x_prompt.dtype), mod_w[l], mod_b[l])
        ms = adaln(c, mod_w[l], mod_b[l])
        xp = ffn_half(xp, mp, 0, norm_g[l, 0], ffn_w_gate[l, 0], ffn_w_up[l, 0], ffn_w_down[l, 0])
        xs = ffn_half(xs, ms, 0, norm_g[l, 0], ffn_w_gate[l, 0], ffn_w_up[l, 0], ffn_w_down[l, 0])
        hp = modulate(xp, norm_g[l, 1], mp[:, :, 3], mp[:, :, 4])
        hs = modulate(xs, norm_g[l, 1], ms[:, :, 3], ms[:, :, 4])
        i = l // 2
        if l % 2 == 0:
            lam_init = 0.8 - 0.6 * math.exp(-0.3 * l)
            qn, qr, ckv, krope, qd, kd, vd = even_project(hp, even_w_in[i], mla_q_norm[i], mla_w_uq[i], mla_kv_norm[i])
            op = even_mix(qn, qr, ckv, krope, qd, kd, vd, mla_w_ukv[i], diff_lambda[i], diff_subln[i],
                          even_w_out[i], lam_init)
            new_ckv.append(ckv)
            new_krope.append(krope)
            new_dk.append(kd)
            new_dv.append(vd)
            qn, qr, ckv, krope, qd, kd, vd = even_project(hs, even_w_in[i], mla_q_norm[i], mla_w_uq[i], mla_kv_norm[i])
            qr = rope_2d(qr, row, col)
            krope = rope_2d(krope, row, col)
            qd = rope_2d(qd.reshape(b_s, t_s, H_B, 2, DH_B), row, col).reshape(b_s, t_s, H_B, 2 * DH_B)
            kd = rope_2d(kd.reshape(b_s, t_s, H_B, 2, DH_B), row, col).reshape(b_s, t_s, H_B, 2 * DH_B)
            os_ = even_mix(qn, qr,
                           jnp.concatenate([cache_mla_ckv[:, i], ckv], axis=1),
                           jnp.concatenate([cache_mla_krope[:, i], krope], axis=1),
                           qd,
                           jnp.concatenate([cache_diff_k[:, i], kd], axis=1),
                           jnp.concatenate([cache_diff_v[:, i], vd], axis=1),
                           mla_w_ukv[i], diff_lambda[i], diff_subln[i], even_w_out[i], lam_init)
        else:
            gla, ret = odd_project(hp, odd_w_in[i], gla_w_gate[i], gla_b_gate[i], ret_decay[i])
            s_gla0 = jnp.zeros((b_p, 2, H_C, DK_C, DV_C), dtype=hp.dtype)
            s_ret0 = jnp.zeros((b_p, 2, H_D, DK_D, DV_D), dtype=hp.dtype)
            op, sg, sr = odd_mix(gla, ret, s_gla0, s_ret0, gla_norm[i], ret_norm[i], odd_w_out[i])
            new_sg.append(sg)
            new_sr.append(sr)
            gla, ret = odd_project(hs, odd_w_in[i], gla_w_gate[i], gla_b_gate[i], ret_decay[i])
            rq, rk, rv, g_ret, rr = ret
            ret = (rope_1d(rq, tpos), rope_1d(rk, tpos), rv, g_ret, rr)
            os_, _, _ = odd_mix(gla, ret, state_gla[:, i], state_ret[:, i], gla_norm[i], ret_norm[i], odd_w_out[i])
        xp = xp + mp[:, :, 5] * op
        xs = xs + ms[:, :, 5] * os_
        xp = ffn_half(xp, mp, 6, norm_g[l, 2], ffn_w_gate[l, 1], ffn_w_up[l, 1], ffn_w_down[l, 1])
        xs = ffn_half(xs, ms, 6, norm_g[l, 2], ffn_w_gate[l, 1], ffn_w_up[l, 1], ffn_w_down[l, 1])

    y_prompt = rmsnorm(xp, final_g)
    y_sample = rmsnorm(xs, final_g)
    return (y_prompt, y_sample, jnp.stack(new_ckv, axis=1), jnp.stack(new_krope, axis=1),
            jnp.stack(new_dk, axis=1), jnp.stack(new_dv, axis=1),
            jnp.stack(new_sg, axis=1), jnp.stack(new_sr, axis=1))


_drawn_inputs = setup_inputs


def setup_inputs(seed=0):
    import zlib

    import numpy as np

    out = dict(_drawn_inputs(seed))
    spreads = {}
    factors = {'cache_mla_ckv': 3.66,
     'cache_mla_krope': 7.029,
     'state_gla': 8.0,
     'mla_q_norm': 8.0,
     'mla_kv_norm': 2.972,
     'diff_subln': 6.143,
     'gla_norm': 8.0,
     'ret_norm': 8.0,
     'final_g': 2.908}
    for name, (base, spread) in spreads.items():
        noise = np.random.default_rng([zlib.crc32(name.encode()), seed]).standard_normal(out[name].shape)
        drawn = base * np.exp(spread * noise) if base else spread * noise
        out[name] = __import__('jax').numpy.asarray(drawn.astype(out[name].dtype))
    for name, factor in factors.items():
        out[name] = (out[name] * factor).astype(out[name].dtype)
    return out
```

```python
import math
from contextlib import ExitStack

import numpy as np
import concourse.bass as bass
from concourse import mybir

F32 = mybir.dt.float32
F32R = mybir.dt.float32r
ALU = mybir.AluOpType
ACT = mybir.ActivationFunctionType
AX = mybir.AxisListType

P = 128
D = 1024
DT = D // P
T_LAT, T_CTX = 512, 128
TOK = T_LAT + T_CTX
PAST = 128
KEYS = PAST + TOK
DEPTH, N_MOD = 2, 9
D_FF = 2816
FT = D_FF // P
PAIR = 2 * P
FIRST_PAIRS, SECOND_PAIRS = 6, 5
HALF_TILES = (2 * FIRST_PAIRS, 2 * SECOND_PAIRS)
UNIT = DT * PAIR
EPS = 1e-6
H_A, NOPE_A, ROPE_A, V_A = 8, 64, 32, 64
Q_LORA, KV_LORA = 384, 256
H_B, DH_B = 4, 64
DV_B = 2 * DH_B
H_C, DK_C, DV_C = 4, 64, 128
H_D, DK_D, DV_D = 4, 64, 128
GATE_RANK, GATE_TAU = 16, 16.0
GRID_W = 64
ROPE_BASE = 10000.0
CHUNK = 128
N_CHUNK = TOK // CHUNK
LAM_INIT = 0.8 - 0.6 * math.exp(0.0)

RUN_A, RUN_B = (0, 384), (384, TOK)
CONDS = ((0, T_LAT, 0), (T_LAT, TOK, 1))
COND_PIECES = ((0, 384, 0), (384, 512, 0), (512, 640, 1))

ROWS = {}
_at = 0
for _name, _n in (("norm_g", DEPTH * 3 * DT), ("final_g", DT), ("c", DT), ("c_ctx", DT), ("mla_q_norm", 3),
                  ("mla_kv_norm", 2), ("diff_subln", 1), ("gla_norm", 1), ("ret_norm", 1), ("gla_b_gate", 4)):
    ROWS[_name] = (_at, _n)
    _at += _n
N_ROWS = _at
MOD_ROWS = DEPTH * N_MOD * DT

FFN_UNITS = 2 * FIRST_PAIRS + 8 + 2 * SECOND_PAIRS + 8
EVEN_T = (0, 256, 512, 672, 928, 1184, 1440)
EVEN_TOK = (1696, 1952)
ODD_T = (0, 256, 1056, 1312, 1568, 1824, 2592, 2848)
ODD_TOK = (512, 768, 2080, 2336)
GLR_COLUMN = 1024
OUT_UNITS = D // PAIR
EVEN_UNITS = len(EVEN_T) + len(EVEN_TOK) + 3 + OUT_UNITS
ODD_UNITS = 1 + len(ODD_T) + len(ODD_TOK) + OUT_UNITS
PHASE_UNITS = {"ffn0": FFN_UNITS, "even": EVEN_UNITS, "ffn1": FFN_UNITS, "ffn2": FFN_UNITS, "odd": ODD_UNITS, "ffn3": FFN_UNITS}
PHASES = ("ffn0", "even", "ffn1", "ffn2", "odd", "ffn3")

MOD_UNITS = DEPTH * N_MOD * 4
MOD_HEAD = 8
MOD_PLAN = {0: (12, 8, 10, 0), 1: (12, 8, 10, 0), 2: (4, 0, 0, 0), 3: (0, 0, 0, 0)}
MOD_BASE = {}
_at = MOD_HEAD
for _f in range(4):
    for _s in range(4):
        MOD_BASE[_f, _s] = _at
        _at += MOD_PLAN[_f][_s]
assert _at == MOD_UNITS

SHIFT_OF = {"ffn0": 0, "even": 3, "ffn1": 6, "ffn2": 9, "odd": 12, "ffn3": 15}


def flat(ap):
    return ap.rearrange("p a b -> p (a b)")


class Steps:

    def __init__(self, engine, semaphore):
        self.engine, self.semaphore, self.n = engine, semaphore, 0

    def mark(self, instruction):
        instruction.then_inc(self.semaphore, 1)
        self.n += 1
        return instruction

    def wait(self, back=0):
        self.engine.wait_ge(self.semaphore, self.n - back)

    def link(self, instruction):
        self.mark(instruction)
        self.wait()


def build(nc, a, phases=PHASES):
    unit_base, n_units = {}, 0
    for name in phases:
        unit_base[name] = n_units
        n_units += PHASE_UNITS[name]
    norm_of = {name: r for r, name in enumerate(phases)}
    norm_of["final"] = len(phases)

    ctx = ExitStack()
    top = [0]

    def sb(name, shape, dt=F32):
        nbytes = 4 * int(np.prod(shape[1:]))
        t = nc.alloc_sbuf_tensor_at(name, list(shape), dt, offset=SB0 + top[0])
        at = top[0]
        top[0] += (nbytes + 31) // 32 * 32
        return t, at

    def view(name, shape, at, end, dt=F32):
        nbytes = 4 * int(np.prod(shape[1:]))
        assert at + nbytes <= end, (name, at + nbytes, end)
        return nc.alloc_sbuf_tensor_at(name, list(shape), dt, offset=SB0 + at), at + (nbytes + 31) // 32 * 32

    SB0 = (nc.sbuf_base + 31) // 32 * 32

    x, _ = sb("x", [P, DT, TOK])
    hh, at_h = sb("hh", [P, DT, TOK], F32R)
    hl, _ = sb("hl", [P, DT, TOK], F32R)
    end_h = top[0]
    ah, at_a = sb("ah", [P, HALF_TILES[0], TOK], F32R)
    al, _ = sb("al", [P, HALF_TILES[0], TOK], F32R)
    end_a = top[0]
    raw, _ = sb("raw", [P, 2, UNIT])
    wh, _ = sb("wh", [P, 2, UNIT], F32R)
    wl, _ = sb("wl", [P, 2, UNIT], F32R)
    mraw, at_m = sb("mraw", [P, 2, DT, PAIR])
    macc, _ = sb("macc", [P, 2, 2, PAIR])
    end_m = top[0]
    sg, at_sg = sb("sg", [P, 2, TOK])
    af, _ = sb("af", [P, 2, TOK])
    ssum, _ = sb("ssum", [P, TOK])
    rstd = ssum
    mod, _ = sb("mod", [P, 2, MOD_ROWS])
    mred, _ = sb("mred", [P, 2, 2])
    modb, _ = sb("modb", [P, MOD_ROWS])
    vec, _ = sb("vec", [P, N_ROWS])
    cs, _ = sb("cs", [P, DT, 2])
    g1, _ = sb("g1", [P, 2, DT])
    hgate, _ = sb("hgate", [P, 2, DT])
    ident, _ = sb("ident", [P, P])
    ones, _ = sb("ones", [P, P])
    rot, _ = sb("rot", [P, 3, P])
    eps, _ = sb("eps", [P, 1])
    assert SB0 + top[0] <= nc.sbuf_usable_end, (SB0 + top[0])

    psG = ctx.enter_context(nc.psum_tensor("psG", [P, 3, 512], F32))
    psU = ctx.enter_context(nc.psum_tensor("psU", [P, 3, 512], F32))
    psA = ctx.enter_context(nc.psum_tensor("psA", [P, 512], F32))
    psB = ctx.enter_context(nc.psum_tensor("psB", [P, 512], F32))
    banks = [psG[:, 0, :], psG[:, 1, :], psG[:, 2, :], psU[:, 0, :], psU[:, 1, :], psU[:, 2, :], psA[:, :], psB[:, :]]

    xin, _ = view("xin", [P, TOK // P, D], at_a, end_a)
    rows, at = view("rows", [P, P], at_h, end_h)
    brows, at = view("brows", [P, 2, P], at, end_h)
    mshift, _ = view("mshift", [P, DT, D], at_a + 4 * (TOK // P) * D, end_a)
    mscale, _ = view("mscale", [P, DT, D], at, end_h)
    mrow, _ = view("mrow", [2, 2 * D], at_a + 4 * (TOK // P + DT) * D, end_a)
    nf, _ = view("nf", [P, 4, TOK], at_sg, at_sg + 4 * 4 * TOK)
    yout, _ = view("yout", [P, TOK // P, D], at_a, end_a)

    names = set()

    def sem(name):
        assert name not in names
        names.add(name)
        return ctx.enter_context(nc.semaphore(name))

    start_in = sem("start_in")
    x_in = sem("x_in")
    raw_in = [sem("raw_in0"), sem("raw_in1")]
    head_in = [sem("shift_in"), sem("scale_in")]
    head_mm, mrow_ok = sem("head_mm"), sem("mrow_ok")
    mod_in = [sem("mod_in0"), sem("mod_in1")]
    stored = sem("stored")
    const_ok = sem("const_ok")
    w_hi, w_lo = sem("w_hi"), sem("w_lo")
    w_used = sem("w_used")
    macc_ok = sem("macc_ok")
    mturn_ok = sem("mturn_ok")
    mred_ok = sem("mred_ok")
    gate_mm, up_mm = sem("gate_mm"), sem("up_mm")
    silu_ok = sem("silu_ok")
    prod_ok = sem("prod_ok")
    a_hi, a_lo = sem("a_hi"), sem("a_lo")
    down_mm = [sem("down_mm0"), sem("down_mm1")]
    res_ok = [sem("res_ok0"), sem("res_ok1")]
    sq_ok = sem("sq_ok")
    ssum_ok = sem("ssum_ok")
    ms_ok = sem("ms_ok")
    rms_ok = sem("rms_ok")
    hf_ok = sem("hf_ok")
    h_hi = sem("h_hi")
    h_lo = [sem("h_lo_dve"), sem("h_lo_pool")]
    turn_mm = sem("turn_mm")
    turn_dve, turn_act = sem("turn_dve"), sem("turn_act")
    cs_ok = sem("cs_ok")
    dve_steps, act_steps, pool_steps = sem("dve_steps"), sem("act_steps"), sem("pool_steps")

    def tile_of(t, index, lo=0, hi=TOK):
        return flat(t[:, bass.ds(index, 1), lo:hi]) if not isinstance(index, int) else t[:, index, lo:hi]

    def runs_of(ps, m):
        return ((RUN_A, ps[:, 1 + m, 0:384]), (RUN_B, ps[:, 0, m * 256:(m + 1) * 256]))

    def runs_alone(ps):
        return runs_of(ps, 0)

    pair_end = {1: FIRST_PAIRS, 3: FIRST_PAIRS + SECOND_PAIRS}
    res_base, used_base = {}, {}
    n_res = n_used = 0
    for name in phases:
        if name.startswith("ffn"):
            for part in (1, 3):
                res_base[int(name[3]), part], used_base[int(name[3]), part] = n_res, n_used
                n_res, n_used = n_res + 4, n_used + 4
        else:
            res_base[name] = n_res
            n_res += 4
    PER_MOD = 32
    n_mixer_stores = 4 * ("even" in phases) + 2 * ("odd" in phases)

    def ffn_parts(f):
        base = unit_base[f"ffn{f}"]
        return ((0, base, FIRST_PAIRS, 0), (1, base + 12, 4, 0), (2, base + 20, SECOND_PAIRS, FIRST_PAIRS),
                (3, base + 30, 4, 0))

    def input_split(engine, r, k=DT - 1):
        engine.wait_ge(h_lo[0], DT // 2 * r + k // 2 + 1)
        if k:
            engine.wait_ge(h_lo[1], DT // 2 * r + (k + 1) // 2)

    def turns(engine, lo, hi, body, apart=False):
        if apart:
            body(lo)
            lo += 1
        if lo < hi:
            with engine.Fori(lo, hi) as i:
                body(i)

    def passed(engine, semaphore, value):
        if not (isinstance(value, int) and value == 0):
            engine.wait_ge(semaphore, value)

    proj_mm = [sem("proj_mm0"), sem("proj_mm1")]
    proj_ok = [sem("proj_ok_act"), sem("proj_ok_dve")]
    tok_mm = sem("tok_mm")
    tok_ok = [sem("tok_ok_act"), sem("tok_ok_dve")]
    o_ok = sem("o_ok")
    o_hi, o_lo = sem("o_hi"), sem("o_lo")
    proj_n = {"even": (0, 0, 0), "odd": ((len(EVEN_T), 5 * len(EVEN_TOK), DT) if "even" in phases else (0, 0, 0))}
    mods_at, _n = {}, MOD_HEAD
    for name in phases:
        mods_at[name] = _n
        _n += sum(MOD_PLAN[int(name[3])]) if name.startswith("ffn") else 0

    def turned_unit_pe(pe, unit_tile, n0, done, r, i=0, step=1, second_bank=None):
        pe.wait_ge(w_lo, (i * step) + (n0 + 1))
        for m in range(2):
            if m and second_bank is not None:
                pe.wait_ge(second_bank, 1)
            if not isinstance(i, int) or done:
                pe.wait_ge(proj_ok[m], (i * step) + done)
            unit_tile(n0 % 2, m, DT, hh, hl, 0, runs_alone((psG, psU)[m]), True, True,
                      (lambda k: input_split(pe, r, k)) if m == 0 else None).then_inc(proj_mm[m], 1)

    def tok_unit_pe(pe, n0, done, i=0):
        pe.wait_ge(w_lo, (i * 2) + (n0 + 1))
        slot = n0 % 2
        for j in range(TOK // P):
            c = done + j
            if c >= 2 or not isinstance(i, int):
                pe.wait_ge(tok_ok[c % 2], (i * 5) + c // 2)
            ps = (psG, psU)[c % 2][:, 2, 0:PAIR]
            tokens = slice(j * P, (j + 1) * P)
            for k in range(DT):
                w = slice(k * PAIR, (k + 1) * PAIR)
                nc.tensor.matmul(ps, hh[:, k, tokens], wh[:, slot, w], start=k == 0, stop=False)
                nc.tensor.matmul(ps, hh[:, k, tokens], wl[:, slot, w], start=False, stop=False)
                ins = nc.tensor.matmul(ps, hl[:, k, tokens], wh[:, slot, w], start=False, stop=k == DT - 1)
            ins.then_inc(tok_mm, 1)

    def turned_out(eng, copy, m, tile, done):
        eng.wait_ge(proj_mm[m], done + 1)
        for (lo, hi), ps in runs_alone((psG, psU)[m]):
            ins = copy(tile[:, lo:hi], ps)
        ins.then_inc(proj_ok[m], 1)

    def tok_out(eng, copy, dst, c):
        eng.wait_ge(tok_mm, c + 1)
        copy(dst, (psG, psU)[c % 2][:, 2, 0:PAIR]).then_inc(tok_ok[c % 2], 1)

    def out_load(sp, load_unit, w, base, first=0, end=OUT_UNITS // 2):
        src = a[w].rearrange("n (k p) c -> p (n k) c", p=P)
        with sp.Fori(first, end) as i:
            for s in range(2):
                load_unit(i * 2 + (base + s), (base + s) % 2,
                          raw[:, (base + s) % 2].rearrange("p (k c) -> p k c", c=PAIR),
                          src[:, :, bass.ds(i * (2 * PAIR) + s * PAIR, PAIR)])

    def out_pe(pe, unit_tile, name, base):
        o0 = proj_n[name][2]
        with pe.Fori(0, OUT_UNITS // 2) as i:
            for s in range(2):
                pe.wait_ge(w_lo, i * 2 + (base + s + 1))
                for m in range(2):
                    pe.wait_ge(res_ok[m], i * 2 + (res_base[name] + s))
                    unit_tile((base + s) % 2, m, DT, hh, hl, 0, runs_alone((psG, psU)[m]), True, True,
                              (lambda k: pe.wait_ge(o_lo, o0 + k + 1)) if m == 0 else None).then_inc(down_mm[m], 1)

    def out_act(act, split, res_squares, name, base):
        r = norm_of[name] + 1
        last = name == phases[-1]

        def pair(i, s, more):
            o = i * 2 + s
            if more:
                act.wait_ge(down_mm[1], o + (res_base[name] + 1))
                split(base + 2 + s, i)
            for m in range(2):
                res_squares(r, o, m, res_base[name] + 1)
        with act.Fori(0, OUT_UNITS // 2 - last) as i:
            for s in range(2):
                pair(i, s, True)
        if last:
            for s in range(2):
                pair(OUT_UNITS // 2 - 1, s, False)

    def out_pool(pool, split_lo, name, base):
        with pool.Fori(0, OUT_UNITS // 2 - (name == phases[-1])) as i:
            for s in range(2):
                split_lo(i * 2 + (base + 2 + s), (base + s) % 2)

    def out_dve(dve, st, residual, add_squares, gate_of, name, layer):
        gate_of(layer * N_MOD + 5, 1.0, res_base[name])
        st.link(nc.vector.memset(ssum[:], 0.0))
        with dve.Fori(0, OUT_UNITS // 2) as i:
            for s in range(2):
                for m in range(2):
                    residual(i * 2 + s, m, res_base[name])
                for m in range(2):
                    add_squares(i * 2 + s, m, norm_of[name] + 1)

    EB = unit_base.get("even", 0)
    ET, EK = len(EVEN_T), len(EVEN_TOK)
    CQ, CKV, KR, QD, KD = 0, 3, 5, 6, 10
    KEY_TILES = KEYS // P
    proj, at = view("proj", [P, 14, TOK], at_a, end_a)
    vd, at = view("vd", [P, KEY_TILES, H_B * DV_B], at, end_a)
    va, _ = view("va", [P, KEY_TILES, H_A * V_A], at, end_a)
    sq_e, at2 = view("sq_e", [P, 3, TOK], at, end_a)
    rt_e, _ = view("rt_e", [P, TOK], at2, end_a)
    qa, at = view("qa", [96, H_A, TOK], at_h, end_h)
    ch, at = view("ch", [P, 2, KEYS], at, end_h, F32R)
    cl, at = view("cl", [P, 2, KEYS], at, end_h, F32R)
    kdc, at = view("kdc", [P, H_B, PAST], at, end_h)
    krt, at = view("krt", [ROPE_A, KEYS], at, end_h)
    st_ckv, at = view("st_ckv", [P, KV_LORA], at, end_h)
    st_kd, at = view("st_kd", [P, H_B * 2 * DH_B], at, end_h)
    cqh, at = view("cqh", [P, 3, TOK], at_m, end_m, F32R)
    cql, at = view("cql", [P, 3, TOK], at, end_m, F32R)
    cache_c, at = view("cache_c", [P, KV_LORA], at, end_m)
    cache_k, at = view("cache_k", [P, H_B * 2 * DH_B], at, end_m)
    cache_r, at = view("cache_r", [P, ROPE_A], at, end_m)
    pt, at = view("pt", [P, 2, 5, P], at_m, end_m)
    pr, at = view("pr", [P, 2, TOK], at, end_m)
    kt, _ = view("kt", [96, 2, KEYS], at, end_m)
    pr2, _ = view("pr2", [P, 2, TOK], at, end_m)
    tab_d = sg[:, :, :].rearrange("p a b -> p (a b)")[:, 0:2 * T_LAT].rearrange("p (a t) -> p a t", a=2)
    tab_a = af[:, :, :].rearrange("p a b -> p (a b)")[:, 0:2 * T_LAT].rearrange("p (a t) -> p a t", a=2)
    lam_in = af[:, :, :].rearrange("p a b -> p (a b)")[:, 2 * T_LAT:2 * T_LAT + 256]
    lam_pr = sg[:, :, :].rearrange("p a b -> p (a b)")[:, 2 * T_LAT:2 * T_LAT + 128].rearrange("p (a b) -> p a b", a=2)
    st_kr, _ = sb("st_kr", [P, ROPE_A])
    stat, _ = sb("stat", [P, 4, 4])
    lam, _ = sb("lam", [P, 4])
    assert SB0 + top[0] <= nc.sbuf_usable_end
    rope = ssum[:, 0:T_LAT]

    e_in = sem("e_in")
    e_sq, e_sum, e_ms, e_rt = sem("e_sq"), sem("e_sum"), sem("e_ms"), sem("e_rt")
    e_n = sem("e_n")
    e_hi, e_lo = sem("e_hi"), sem("e_lo")
    e_rot = sem("e_rot")
    e_roped = sem("e_roped")
    e_turn = sem("e_turn")
    e_turned = sem("e_turned")
    e_cc = sem("e_cc")
    e_q = sem("e_q")
    e_qo = [sem("e_qo_act"), sem("e_qo_dve")]
    e_v = sem("e_v")
    e_vo = [sem("e_vo_act"), sem("e_vo_dve")]
    e_k = sem("e_k")
    e_ko = [sem("e_ko_act"), sem("e_ko_dve")]
    e_kr = sem("e_kr")
    e_s = sem("e_s")
    e_nb, e_ex = sem("e_nb"), sem("e_ex")
    e_p = sem("e_p")
    e_t, e_to = sem("e_t"), sem("e_to")
    e_pv, e_o = sem("e_pv"), sem("e_o")
    e_lam, e_lexp = sem("e_lam"), sem("e_lexp")
    d_sq, d_ms, d_rt = sem("d_sq"), sem("d_ms"), sem("d_rt")

    A_STEPS = [(h, j) for h in range(H_A) for j in range(5)]
    D_STEPS = [(h, j) for h in range(H_B) for j in range(5)]
    NA = len(A_STEPS)
    ROPED = [QD, QD + 1, QD + 2, QD + 3, KD, KD + 1, KD + 2, KD + 3]

    def buffers(n):
        return (psG, psU)[n % 2][:, 0:2, :].rearrange("p a b -> p (a b)")

    def n_keys(j):
        return 640 if j < 4 else P

    def even_load(sp, load_unit):
        w = a["even_w_in"].rearrange("n (k p) c -> p (n k) c", p=P)

        def whole(n, src):
            load_unit(n, n % 2, raw[:, n % 2, 0:src.shape[1] * src.shape[2]].rearrange("p (k c) -> p k c", c=src.shape[2]), src)
        for u, c in enumerate(EVEN_T + EVEN_TOK):
            whole(EB + u, w[:, :, c:c + PAIR])
            if u == 2:
                input_split(sp, norm_of["even"])
                sp.wait_ge(mred_ok, mods_at["even"])
                sp.dma_start(tab_a, a["rope_tables"][0]).then_inc(e_in, 16)
                sp.dma_start(tab_d, a["rope_tables"][1]).then_inc(e_in, 16)
                sp.dma_start(lam_in, a["diff_lambda"].rearrange("n a b -> n (a b)").to_broadcast([P, 256])).then_inc(e_in, 16)
                sp.dma_start(cache_c[:], a["cache_mla_ckv"].rearrange("b n t c -> (b n t) c")).then_inc(e_in, 16)
                sp.dma_start(cache_r[:], a["cache_mla_krope"].rearrange("b n t c -> (b n t) c")).then_inc(e_in, 16)
                sp.dma_start(cache_k[:], a["cache_diff_k"].rearrange("b n t h c -> (b n t) (h c)")).then_inc(e_in, 16)
                sp.dma_start(vd[:, 0, :], a["cache_diff_v"].rearrange("b n t h c -> (b n t) (h c)")).then_inc(e_in, 16)
        uq = a["mla_w_uq"].rearrange("n (k p) c -> p (n k) c", p=P)
        for u in range(2):
            whole(EB + ET + EK + u, uq[:, :, u * 384:(u + 1) * 384])
        whole(EB + ET + EK + 2, a["mla_w_ukv"].rearrange("n (k p) c -> p (n k) c", p=P))
        sp.wait_ge(e_turned, 4)
        sp.dma_start(a["new_mla_ckv"].rearrange("b n t c -> (b n t) c"), st_ckv[:]).then_inc(stored, 16)
        sp.dma_start(a["new_mla_krope"].rearrange("b n t c -> (b n t) c"), st_kr[:]).then_inc(stored, 16)
        sp.dma_start(a["new_diff_k"].rearrange("b n t h c -> (b n t) (h c)"), st_kd[:]).then_inc(stored, 16)
        sp.dma_start(a["new_diff_v"].rearrange("b n t h c -> (b n t) (h c)"), vd[:, 5, :]).then_inc(stored, 16)
        out_load(sp, load_unit, "even_w_out", EB + ET + EK + 3)

    def even_pool(pool, st, split_lo):
        n = EB + 2
        for u in range(4):
            split_lo(n, n % 2)
            n += 1
        for k in range(3):
            pool.wait_ge(e_hi, k + 1)
            nc.gpsimd.tensor_tensor(cql[:, k], proj[:, CQ + k], cqh[:, k].bitcast(F32), ALU.subtract).then_inc(e_lo, 1)
        for u in range(4, ET + EK):
            split_lo(n, n % 2)
            n += 1
        for k in range(2):
            pool.wait_ge(e_hi, 3 + k + 1)
            nc.gpsimd.tensor_tensor(cl[:, k, PAST:KEYS], proj[:, CKV + k], ch[:, k, PAST:KEYS].bitcast(F32),
                                    ALU.subtract).then_inc(e_lo, 1)
        for u in range(2):
            split_lo(n, n % 2)
            n += 1
        split_lo(n, n % 2)
        for k in range(DT):
            if k == 4:
                pool.wait_ge(e_s, NA + 2 * len(D_STEPS))
                pool.wait_ge(stored, 16 * 4)
            pool.wait_ge(o_hi, proj_n["even"][2] + k + 1)
            nc.gpsimd.tensor_tensor(hl[:, k], proj[:, HEAD_TILES[k]], hh[:, k].bitcast(F32), ALU.subtract).then_inc(o_lo, 1)
        out_pool(pool, split_lo, "even", EB + ET + EK + 3)

    HEAD_TILES = (0, 1, 2, 3, QD, QD + 1, QD + 2, QD + 3)

    def even_act(act, st, split, res_squares):
        copy = nc.scalar.copy

        def root(which, size):
            act.wait_ge(e_ms, which + 1)
            nc.scalar.activation(rt_e[:, 0:384], psA[:, 0:384], ACT.Ln, bias=eps[:], scale=D / size)
            st.link(nc.scalar.activation(rt_e[:, 384:TOK], psB[:, 0:256], ACT.Ln, bias=eps[:], scale=D / size))
            nc.scalar.activation(rt_e[:], rt_e[:], ACT.Exp, scale=-0.5).then_inc(e_rt, 1)

        n = EB + 2
        for u in range(ET):
            turned_out(act, copy, 0, proj[:, 2 * u], u)
            act.wait_ge(proj_mm[1], u + 1)
            split(n)
            n += 1
            if u == 2:
                act.wait_ge(proj_ok[0], 3)
                act.wait_ge(proj_ok[1], 3)
                for k in range(3):
                    nc.scalar.activation(sq_e[:, k], proj[:, CQ + k], ACT.Square).then_inc(e_sq, 1)
            if u == 3:
                root(0, Q_LORA)
                for k in range(3):
                    act.wait_ge(e_n, k + 1)
                    copy(cqh[:, k], proj[:, CQ + k]).then_inc(e_hi, 1)
                for k in range(2):
                    nc.scalar.activation(sq_e[:, k], proj[:, CKV + k], ACT.Square).then_inc(e_sq, 1)
            if u == 4:
                root(1, KV_LORA)
        for u in range(EK):
            for j in range(5):
                c = 5 * u + j
                if c % 2 == 0:
                    tok_out(act, copy, vd[:, j + 1, u * PAIR:(u + 1) * PAIR], c)
            act.wait_ge(tok_mm, 5 * (u + 1))
            split(n)
            n += 1
        for k in range(2):
            act.wait_ge(e_n, 3 + k + 1)
            copy(ch[:, k, PAST:KEYS], proj[:, CKV + k]).then_inc(e_hi, 1)
        act.wait_ge(e_lam, 1)
        nc.scalar.activation(lam[:, 2:4], lam[:, 0:2], ACT.Exp).then_inc(e_lexp, 1)
        act.wait_ge(e_turn, 1)
        copy(ch[:, :, 0:PAST], psA[:, 0:2 * P].rearrange("p (k t) -> p k t", k=2)).then_inc(e_cc, 1)
        for h in range(H_A):
            act.wait_ge(e_q, h + 1)
            if h in (3, 7):
                split(n)
                n += 1
            if h % 2 == 0:
                copy(qa[:, h, 0:384], psG[0:96, 1, 0:384])
                copy(qa[:, h, 384:TOK], psG[0:96, 0, 0:256]).then_inc(e_qo[0], 1)
        act.wait_ge(e_roped, 9 + H_A)
        for t in range(KEY_TILES):
            if t % 2 == 0:
                act.wait_ge(e_v, t + 1)
                copy(va[:, t], psG[:, 2, :]).then_inc(e_vo[0], 1)

        def keys_out(h):
            act.wait_ge(e_k, 2 * h + 1)
            copy(kt[0:NOPE_A, h % 2, 0:384], psA[0:NOPE_A, 0:384]).then_inc(e_ko[0], 1)

        def head_hi(k):
            act.wait_ge(o_ok, proj_n["even"][2] + k + 1)
            copy(hh[:, k], proj[:, HEAD_TILES[k]]).then_inc(o_hi, 1)

        def exponentials(s, scale, dst, j):
            act.wait_ge(e_nb, s + 1)
            nc.scalar.activation(dst[:, 0:n_keys(j)], buffers(s)[:, 0:n_keys(j)], ACT.Exp, bias=stat[:, 1, s % 4:s % 4 + 1],
                                 scale=scale, accum_out=stat[:, 2, s % 4:s % 4 + 1]).then_inc(e_ex, 1)

        def turned(n, j):
            act.wait_ge(e_t, n + 1)
            k = n_keys(j) // P
            if k == 5:
                copy(pt[:, n % 2, 4], psU[:, 2, 0:P])
            copy(pt[:, n % 2, 0:min(k, 4)], psG[:, 2, 0:min(k, 4) * P].rearrange("p (k t) -> p k t", t=P)).then_inc(e_to, 1)

        keys_out(0)
        for s, (h, j) in enumerate(A_STEPS):
            if s >= 2:
                act.wait_ge(e_t, s - 1)
            exponentials(s, float(NOPE_A + ROPE_A) ** -0.5, pr[:, s % 2], j)
            if j == 3 and h + 1 < H_A:
                keys_out(h + 1)
            if s >= 1:
                turned(s - 1, A_STEPS[s - 1][1])
        turned(NA - 1, 4)
        act.wait_ge(e_k, 2 * H_A)
        split(n)
        n += 1
        for i, (h, j) in enumerate(D_STEPS):
            for two in range(2):
                s = NA + 2 * i + two
                if i >= 2:
                    act.wait_ge(e_t, NA + i - 1)
                exponentials(s, float(DH_B) ** -0.5, (pr, pr2)[two][:, i % 2], j)
            if i >= 1:
                turned(NA + i - 1, D_STEPS[i - 1][1])
            if i in (8, 13, 18):
                diff_norm_act(act, st, (i - 8) // 5)
            if 2 <= i < 6:
                head_hi(i - 2)
            if i in (11, 16):
                head_hi(4 + (i - 11) // 5)
        turned(NA + len(D_STEPS) - 1, 4)
        diff_norm_act(act, st, 3)
        for k in (6, 7):
            head_hi(k)
        out_act(act, split, res_squares, "even", EB + ET + EK + 3)

    def diff_norm_act(act, st, h):
        act.wait_ge(e_o, NA + 5 * (h + 1))
        if h:
            act.wait_ge(d_ms, h)
        nc.scalar.activation(af[:, 0], proj[:, QD + h], ACT.Square).then_inc(d_sq, 1)
        act.wait_ge(d_ms, h + 1)
        if h:
            act.wait_ge(o_ok, 4 + h)
        nc.scalar.activation(af[:, 1, 0:384], psA[:, 0:384], ACT.Ln, bias=eps[:], scale=D / DV_B)
        st.link(nc.scalar.activation(af[:, 1, 384:TOK], psB[:, 0:256], ACT.Ln, bias=eps[:], scale=D / DV_B))
        nc.scalar.activation(af[:, 1], af[:, 1], ACT.Exp, scale=-0.5).then_inc(d_rt, 1)

    def even_dve(dve, st, residual, add_squares, gate_of):
        copy = nc.vector.tensor_copy

        def normed(which, first, n, gain):
            dve.wait_ge(e_rt, which + 1)
            for k in range(n):
                nc.vector.scalar_tensor_tensor(out=proj[:, first + k], in0=proj[:, first + k],
                                               scalar=vec[:, gain + k:gain + k + 1], in1=rt_e[:],
                                               op0=ALU.mult, op1=ALU.mult).then_inc(e_n, 1)

        def sum_of(n, done):
            dve.wait_ge(e_sq, done + 2)
            if done:
                dve.wait_ge(e_n, done)
            ins = nc.vector.tensor_tensor(ssum[:], sq_e[:, 0], sq_e[:, 1], ALU.add)
            if n == 3:
                st.link(ins)
                dve.wait_ge(e_sq, done + 3)
                ins = nc.vector.tensor_tensor(ssum[:], ssum[:], sq_e[:, 2], ALU.add)
            ins.then_inc(e_sum, 1)

        def roped(count, rows, tile, table, out=None):
            out = tile if out is None else out
            dve.wait_ge(e_rot, count + 1)
            st.link(nc.vector.tensor_tensor(rope[rows], (psA, psB)[count % 2][rows, 0:T_LAT], table[rows, 1], ALU.mult))
            st.link(nc.vector.tensor_tensor(out, tile, table[rows, 0], ALU.mult))
            nc.vector.tensor_tensor(out, out, rope[rows], ALU.add).then_inc(e_roped, 1)
            dve.wait_ge(e_roped, count + 1)

        input_split(dve, norm_of["even"])
        for u in range(ET):
            turned_out(dve, copy, 1, proj[:, 2 * u + 1], u)
            if u == 2:
                sum_of(3, 0)
            if u == 3:
                normed(0, CQ, 3, ROWS["mla_q_norm"][0])
                sum_of(2, 3)
            if u == 4:
                normed(1, CKV, 2, ROWS["mla_kv_norm"][0])
                dve.wait_ge(e_n, 5)
                dve.wait_ge(e_in, 7 * 16)
            if u in (5, 6):
                for t in range(2):
                    c = 2 * (u - 5) + t
                    roped(c, slice(0, P), proj[:, ROPED[c], 0:T_LAT], tab_d)
        for u in range(EK):
            for j in range(5):
                c = 5 * u + j
                if c % 2 == 1:
                    tok_out(dve, copy, vd[:, j + 1, u * PAIR:(u + 1) * PAIR], c)
            for t in range(2):
                c = 4 + 2 * u + t
                roped(c, slice(0, P), proj[:, ROPED[c], 0:T_LAT], tab_d)
        dve.wait_ge(tok_mm, 5 * EK)
        roped(8, slice(0, ROPE_A), proj[0:ROPE_A, KR, 0:T_LAT], tab_a[:], krt[:, PAST:PAST + T_LAT])
        copy(krt[:, PAST + T_LAT:KEYS], proj[0:ROPE_A, KR, T_LAT:TOK])
        pairs = lam_in.rearrange("p (a b c) -> p a b c", a=2, b=2)
        st.link(nc.vector.tensor_tensor(lam_pr, pairs[:, :, 0], pairs[:, :, 1], ALU.mult))
        nc.vector.tensor_reduce(lam[:, 0:2], lam_pr, AX.X, ALU.add).then_inc(e_lam, 1)
        dve.wait_ge(e_lexp, 1)
        st.link(nc.vector.tensor_tensor(lam[:, 0:1], lam[:, 3:4], lam[:, 2:3], ALU.subtract))
        st.link(nc.vector.tensor_scalar(lam[:, 1:2], lam[:, 0:1], -LAM_INIT, None, ALU.add))
        dve.wait_ge(e_cc, 1)
        nc.vector.tensor_tensor(cl[:, :, 0:PAST], psA[:, 0:2 * P].rearrange("p (k t) -> p k t", k=2),
                                ch[:, :, 0:PAST].bitcast(F32), ALU.subtract)
        copy(krt[:, 0:PAST], psA[0:ROPE_A, 2 * P:3 * P]).then_inc(e_turned, 1)
        dve.wait_ge(e_turn, 2)
        copy(kdc[:], psB[:].rearrange("p (k t) -> p k t", t=P)).then_inc(e_turned, 1)
        dve.wait_ge(e_turn, 3)
        copy(st_ckv[:], psG[:, 2, 0:2 * P])
        copy(st_kr[:], psG[:, 2, 2 * P:2 * P + ROPE_A]).then_inc(e_turned, 1)
        dve.wait_ge(e_turn, 4)
        copy(st_kd[:], psU[:, 2, :]).then_inc(e_turned, 1)
        for h in range(H_A):
            if h % 2 == 1:
                dve.wait_ge(e_q, h + 1)
                copy(qa[:, h, 0:384], psU[0:96, 1, 0:384])
                copy(qa[:, h, 384:TOK], psU[0:96, 0, 0:256]).then_inc(e_qo[1], 1)
                dve.wait_ge(e_qo[1], (h + 1) // 2)
                for g in (h - 1, h):
                    dve.wait_ge(e_qo[0], g // 2 + 1)
                    roped(9 + g, slice(64, 96), qa[64:96, g, 0:T_LAT], tab_a)
        dve.wait_ge(e_lo, 3)
        dve.wait_ge(e_turned, 4)
        dve.wait_ge(e_q, H_A)
        for b in range(2):
            ins = copy(kt[64:96, b], krt[:])
        ins.then_inc(e_kr, 1)
        for t in range(KEY_TILES):
            if t % 2 == 1:
                dve.wait_ge(e_v, t + 1)
                copy(va[:, t], psU[:, 2, :]).then_inc(e_vo[1], 1)

        def keys_out(h):
            dve.wait_ge(e_k, 2 * h + 2)
            copy(kt[0:NOPE_A, h % 2, 384:KEYS], psB[0:NOPE_A, 0:384]).then_inc(e_ko[1], 1)

        scale_a, scale_d = -float(NOPE_A + ROPE_A) ** -0.5, -float(DH_B) ** -0.5

        def maximum(s, j):
            dve.wait_ge(e_s, s + 1)
            if s >= 4:
                dve.wait_ge(e_ex, s - 3)
            st.link(nc.vector.tensor_reduce(stat[:, 0, s % 4:s % 4 + 1], buffers(s)[:, 0:n_keys(j)], AX.X, ALU.max))
            nc.vector.tensor_scalar(stat[:, 1, s % 4:s % 4 + 1], stat[:, 0, s % 4:s % 4 + 1],
                                    scale_a if s < NA else scale_d, None, ALU.mult).then_inc(e_nb, 1)

        def inverse(s):
            dve.wait_ge(e_ex, s + 1)
            st.link(nc.vector.reciprocal(stat[:, 3, s % 4:s % 4 + 1], stat[:, 2, s % 4:s % 4 + 1]))

        def heads_out(n, j):
            dve.wait_ge(e_pv, n + 1)
            cols = slice(j * P, (j + 1) * P)
            if n < NA:
                h = n // 5
                rows = slice(64 * (h % 2), 64 * (h % 2) + 64)
                copy(proj[rows, h // 2, cols], psB[rows, 384:512]).then_inc(e_o, 1)
            else:
                copy(proj[:, QD + (n - NA) // 5, cols], psB[:, 384:512]).then_inc(e_o, 1)

        def diff_norm(h):
            dve.wait_ge(d_rt, h + 1)
            g = ROWS["diff_subln"][0]
            nc.vector.scalar_tensor_tensor(out=proj[:, QD + h], in0=proj[:, QD + h], scalar=vec[:, g:g + 1], in1=af[:, 1],
                                           op0=ALU.mult, op1=ALU.mult).then_inc(o_ok, 1)

        keys_out(0)
        maximum(0, 0)
        maximum(1, 1)
        for s, (h, j) in enumerate(A_STEPS):
            inverse(s)
            nc.vector.tensor_scalar(pr[:, s % 2, 0:n_keys(j)], pr[:, s % 2, 0:n_keys(j)], stat[:, 3, s % 4:s % 4 + 1],
                                    None, ALU.mult).then_inc(e_p, 1)
            if s >= 2:
                heads_out(s - 2, A_STEPS[s - 2][1])
            if j == 2 and h + 1 < H_A:
                keys_out(h + 1)
            if s + 2 < NA:
                maximum(s + 2, A_STEPS[s + 2][1])
        heads_out(NA - 2, 3)
        heads_out(NA - 1, 4)
        dve.wait_ge(e_o, NA)
        nc.vector.tensor_copy(lam[:, 2:3], lam[:, 1:2]).then_inc(o_ok, 4)
        for two in range(2):
            maximum(NA + two, 0)
        for i, (h, j) in enumerate(D_STEPS):
            s = NA + 2 * i
            inverse(s)
            inverse(s + 1)
            k = n_keys(j)
            p1, p2 = pr[:, i % 2, 0:k], pr2[:, i % 2, 0:k]
            st.mark(nc.vector.tensor_scalar(p1, p1, stat[:, 3, s % 4:s % 4 + 1], None, ALU.mult))
            st.link(nc.vector.tensor_tensor(stat[:, 3, (s + 1) % 4:(s + 1) % 4 + 1],
                                            stat[:, 3, (s + 1) % 4:(s + 1) % 4 + 1], lam[:, 1:2], ALU.mult))
            nc.vector.scalar_tensor_tensor(out=p1, in0=p2, scalar=stat[:, 3, (s + 1) % 4:(s + 1) % 4 + 1], in1=p1,
                                           op0=ALU.mult, op1=ALU.add).then_inc(e_p, 1)
            if i >= 2:
                heads_out(NA + i - 2, D_STEPS[i - 2][1])
            if i + 1 < len(D_STEPS):
                for two in range(2):
                    maximum(s + 2 + two, D_STEPS[i + 1][1])
            if i in (9, 14, 19):
                diff_norm((i - 9) // 5)
        heads_out(NA + len(D_STEPS) - 2, 3)
        heads_out(NA + len(D_STEPS) - 1, 4)
        diff_norm(3)
        dve.wait_ge(o_ok, proj_n["even"][2] + 8)
        out_dve(dve, st, residual, add_squares, gate_of, "even", 0)

    def even_pe(pe, part_products, unit_tile, norm_sum):
        r = norm_of["even"]

        def turn(out, in_, n=P):
            return nc.tensor.transpose(out, in_, ident[0:n, 0:n])

        def sum_over_partitions(which):
            pe.wait_ge(e_sum, which + 1)
            if which:
                pe.wait_ge(e_rt, which)
            nc.tensor.matmul(psA[:, 0:384], ones[:], ssum[:, 0:384], start=True, stop=True)
            nc.tensor.matmul(psB[:, 0:256], ones[:], ssum[:, 384:TOK], start=True, stop=True).then_inc(e_ms, 1)

        def rotate(count, which, rows, tile):
            if count < 2:
                pe.wait_ge(e_rt, 2)
            else:
                pe.wait_ge(e_roped, count - 1)
            nc.tensor.matmul((psA, psB)[count % 2][0:rows, 0:T_LAT], rot[0:rows, which, 0:rows], tile,
                             start=True, stop=True).then_inc(e_rot, 1)

        def both(c):
            for t in (c, c + 1):
                if ROPED[t] % 2:
                    pe.wait_ge(proj_ok[1], ROPED[t] // 2 + 1)
                else:
                    pe.wait_ge(proj_ok[0], ROPED[t] // 2 + 1)
                rotate(t, 1, P, proj[:, ROPED[t], 0:T_LAT])

        for u in range(ET):
            turned_unit_pe(pe, unit_tile, EB + u, u, r)
            if u == 3:
                sum_over_partitions(0)
            if u == 4:
                sum_over_partitions(1)
            if u == 5:
                both(0)
            if u == 6:
                both(2)
        for u in range(EK):
            tok_unit_pe(pe, EB + ET + u, 5 * u)
            both(4 + 2 * u)
        rotate(8, 0, ROPE_A, proj[0:ROPE_A, KR, 0:T_LAT])
        pe.wait_ge(e_roped, 9)
        for k in range(2):
            turn(psA[:, k * P:(k + 1) * P], cache_c[:, k * P:(k + 1) * P])
        turn(psA[0:ROPE_A, 2 * P:3 * P], cache_r[:]).then_inc(e_turn, 1)
        for k in range(H_B):
            ins = turn(psB[:, k * P:(k + 1) * P], cache_k[:, k * P:(k + 1) * P])
        ins.then_inc(e_turn, 1)
        pe.wait_ge(tok_ok[0], 5)
        pe.wait_ge(tok_ok[1], 5)
        pe.wait_ge(e_n, 5)
        for k in range(2):
            turn(psG[:, 2, k * P:(k + 1) * P], proj[:, CKV + k, T_LAT:TOK])
        turn(psG[:, 2, 2 * P:2 * P + ROPE_A], proj[0:ROPE_A, KR, T_LAT:TOK], ROPE_A).then_inc(e_turn, 1)
        for k in range(H_B):
            ins = turn(psU[:, 2, k * P:(k + 1) * P], proj[:, KD + k, T_LAT:TOK])
        ins.then_inc(e_turn, 1)
        for h in range(H_A):
            n = EB + ET + EK + h // 4
            pe.wait_ge(w_lo, n + 1)
            pe.wait_ge(proj_ok[h % 2], ET)
            if h >= 2:
                pe.wait_ge(e_qo[h % 2], h // 2)
            ps = (psG, psU)[h % 2]
            for k in range(3):
                pe.wait_ge(e_lo, k + 1)
                w = slice(k * 384 + (h % 4) * 96, k * 384 + (h % 4 + 1) * 96)
                ins = part_products(wh[:, n % 2, w], wl[:, n % 2, w], cqh[:, k], cql[:, k],
                                    ((RUN_A, ps[0:96, 1, 0:384]), (RUN_B, ps[0:96, 0, 0:256])), k == 0, k == 2)
            ins.then_inc(e_q, 1)
            if h % 2 and h >= 3:
                for g in (h - 3, h - 2):
                    pe.wait_ge(e_qo[g % 2], g // 2 + 1)
                    if g < 2:
                        pe.wait_ge(e_turned, 2)
                    rotate(9 + g, 0, 96, qa[:, g, 0:T_LAT])
        for g in (6, 7):
            pe.wait_ge(e_qo[g % 2], g // 2 + 1)
            rotate(9 + g, 0, 96, qa[:, g, 0:T_LAT])
        n = EB + ET + EK + 2
        slot = n % 2
        pe.wait_ge(w_lo, n + 1)
        pe.wait_ge(e_lo, 5)
        pe.wait_ge(e_turned, 4)
        for t in range(KEY_TILES):
            if t >= 2:
                pe.wait_ge(e_vo[t % 2], t // 2)
            keys = slice(t * P, (t + 1) * P)
            for k in range(2):
                def values(w):
                    return w[:, slot, k * 1024:(k + 1) * 1024].rearrange("p (h two d) -> p h two d", two=2, d=V_A)[:, :, 1]
                ps = (psG, psU)[t % 2][:, 2, :].rearrange("p (h d) -> p h d", d=V_A)
                nc.tensor.matmul(ps, ch[:, k, keys], values(wh), start=k == 0, stop=False)
                nc.tensor.matmul(ps, ch[:, k, keys], values(wl), start=False, stop=False)
                ins = nc.tensor.matmul(ps, cl[:, k, keys], values(wh), start=False, stop=k == 1)
            ins.then_inc(e_v, 1)

        def head_keys(h):
            pe.wait_ge(e_kr, 1)
            if h == 0:
                pe.wait_ge(e_roped, 9 + H_A)
            for half, bank in enumerate((psA, psB)):
                if h:
                    pe.wait_ge(e_ko[half], h)
                if half and h:
                    pe.wait_ge(e_o, key_turn[h] - 1)
                for k in range(2):
                    w = slice(k * 1024 + h * 128, k * 1024 + h * 128 + NOPE_A)
                    keys = slice(half * 384, (half + 1) * 384)
                    ps = bank[0:NOPE_A, 0:384]
                    nc.tensor.matmul(ps, wh[:, slot, w], ch[:, k, keys], start=k == 0, stop=False)
                    nc.tensor.matmul(ps, wh[:, slot, w], cl[:, k, keys], start=False, stop=False)
                    ins = nc.tensor.matmul(ps, wl[:, slot, w], ch[:, k, keys], start=False, stop=k == 1)
                ins.then_inc(e_k, 1)

        key_turn = {}

        def scores_a(s):
            h, j = A_STEPS[s]
            for half in range(2):
                pe.wait_ge(e_ko[half], h + 1)
            if s >= 2:
                pe.wait_ge(e_ex, s - 1)
            q = qa[:, h, j * P:(j + 1) * P]
            if j < 4:
                nc.tensor.matmul(buffers(s)[:, 0:512], q, kt[:, h % 2, 0:512], start=True, stop=True)
                ins = nc.tensor.matmul(buffers(s)[:, 512:640], q, kt[:, h % 2, 512:640], start=True, stop=True)
            else:
                ins = nc.tensor.matmul(buffers(s)[:, 0:P], q, kt[:, h % 2, 640:768], start=True, stop=True)
            ins.then_inc(e_s, 1)

        def turn_p(n, j):
            pe.wait_ge(e_p, n + 1)
            if n >= 1:
                pe.wait_ge(e_to, n)
            src = pr[:, (n if n < NA else n - NA) % 2]
            for k in range(n_keys(j) // P):
                ins = turn(psG[:, 2, k * P:(k + 1) * P] if k < 4 else psU[:, 2, 0:P], src[:, k * P:(k + 1) * P])
            ins.then_inc(e_t, 1)

        def weigh(n, j):
            pe.wait_ge(e_to, n + 1)
            if n >= 1:
                pe.wait_ge(e_o, n)
            if n < NA and A_STEPS[n][1] == 1 and n // 5 + 1 < H_A:
                pe.wait_ge(e_ko[1], n // 5 + 2)
            kn = n_keys(j) // P
            for k in range(kn):
                if n < NA:
                    h = n // 5
                    v = va[:, 5 if j == 4 else k, h * V_A:(h + 1) * V_A]
                    out = psB[64 * (h % 2):64 * (h % 2) + 64, 384:512]
                else:
                    h = (n - NA) // 5
                    v = vd[:, 5 if j == 4 else (k + 1) % 5, h * DV_B:(h + 1) * DV_B]
                    out = psB[:, 384:512]
                ins = nc.tensor.matmul(out, v, pt[:, n % 2, k], start=k == 0, stop=k == kn - 1)
            ins.then_inc(e_pv, 1)

        head_keys(0)
        pe.wait_ge(e_vo[0], 3)
        pe.wait_ge(e_vo[1], 3)
        scores_a(0)
        scores_a(1)
        for s, (h, j) in enumerate(A_STEPS):
            if j == 2 and h + 1 < H_A:
                key_turn[h + 1] = s
                head_keys(h + 1)
            if s + 2 < NA:
                scores_a(s + 2)
            turn_p(s, j)
            if s >= 1:
                weigh(s - 1, A_STEPS[s - 1][1])
        weigh(NA - 1, 4)

        def scores_d(i):
            h, j = D_STEPS[i]
            for two in range(2):
                s = NA + 2 * i + two
                pe.wait_ge(e_ex, s - 1)
                rows = slice(64 * two, 64 * two + 64)
                q = proj[rows, QD + h, j * P:(j + 1) * P]
                if j < 4:
                    nc.tensor.matmul(buffers(s)[:, 0:512], q, proj[rows, KD + h, 0:T_LAT], start=True, stop=True)
                    ins = nc.tensor.matmul(buffers(s)[:, 512:640], q, kdc[rows, h], start=True, stop=True)
                else:
                    ins = nc.tensor.matmul(buffers(s)[:, 0:P], q, proj[rows, KD + h, T_LAT:TOK], start=True, stop=True)
                ins.then_inc(e_s, 1)

        def diff_norm_sum(h):
            pe.wait_ge(d_sq, h + 1)
            if h:
                pe.wait_ge(d_rt, h)
            pe.wait_ge(e_o, NA + (5 * h + 7 if h < 3 else 20))
            nc.tensor.matmul(psA[:, 0:384], ones[:], af[:, 0, 0:384], start=True, stop=True)
            nc.tensor.matmul(psB[:, 0:256], ones[:], af[:, 0, 384:TOK], start=True, stop=True).then_inc(d_ms, 1)

        scores_d(0)
        for i, (h, j) in enumerate(D_STEPS):
            if i + 1 < len(D_STEPS):
                scores_d(i + 1)
            turn_p(NA + i, j)
            if i in (8, 13, 18):
                diff_norm_sum((i - 8) // 5)
                pe.wait_ge(d_rt, (i - 8) // 5 + 1)
            if i >= 1:
                weigh(NA + i - 1, D_STEPS[i - 1][1])
        weigh(NA + len(D_STEPS) - 1, 4)
        diff_norm_sum(3)
        out_pe(pe, unit_tile, "even", EB + ET + EK + 3)

    OB = unit_base.get("odd", 0)
    OT, OK = len(ODD_T), len(ODD_TOK)
    GQ, GK, GR, RQ, RK, RR = 0, 2, 4, 8, 10, 12
    LAT = T_LAT // CHUNK
    feat, at = view("feat", [P, 16, TOK], at_a, end_a)
    gv, at = view("gv", [P, N_CHUNK, H_C * DV_C], at, end_a)
    rv, _ = view("rv", [P, N_CHUNK, H_D * DV_D], at, end_a)
    g4, at = view("g4", [P, 4, TOK], at_m, end_m)
    glr, at2 = view("glr", [2 * GATE_RANK, TOK], at, end_m)
    mret, at3 = view("mret", [P, H_D, CHUNK], at, end_m)
    refv, at3 = view("refv", [P, 4, N_CHUNK], at3, at2)
    totv, at3 = view("totv", [P, 4, N_CHUNK], at3, at2)
    eref, at3 = view("eref", [P, 4, N_CHUNK], at3, at2)
    etot, at3 = view("etot", [P, 4, N_CHUNK], at3, at2)
    etr, at3 = view("etr", [P, 4, N_CHUNK], at3, at2)
    tab_r, at3 = view("tab_r", [P, 2, T_LAT], at2, end_m)
    dist, at4 = view("dist", [P, 4, CHUNK], at2, end_m)
    decq, _ = view("decq", [P, 2, 2, CHUNK], at4, end_m)
    restart, at5 = view("restart", [P, TOK], at3, end_m)
    st_g, _ = view("st_g", [P, 2, 2, DV_C], at3, end_m)
    masks, _ = view("masks", [P, 2, CHUNK], at5, end_m)
    lt, _ = view("lt", [P, 4, TOK], at_sg, at_sg + 4 * 4 * TOK)
    qret, _ = view("qret", [P, 2, 2, T_LAT], at_sg, at_sg + 4 * 4 * TOK)
    kst_g, at = view("kst_g", [P, 2, N_CHUNK, 256], at_h, end_h)
    ss_r, at0 = view("ss_r", [P, 2, LAT, 2, DV_D], at_h, end_h)
    sr_r, _ = view("sr_r", [P, 2, 2, DV_D], at0, at)
    kst_r, at = view("kst_r", [P, 2, N_CHUNK, 256], at, end_h)
    ss_g, at = view("ss_g", [P, 2, LAT, 2, DV_C], at, end_h)
    sr_g, at = view("sr_g", [P, 2, 2, DV_C], at, end_h)
    am, at = view("am", [P, 2, H_C, CHUNK], at, end_h)
    am2, _ = view("am2", [P, 2, 2, 2, CHUNK], at, end_h)
    st_r, _ = view("st_r", [P, 2, 2, DV_D], at, end_h)
    n_sq, at = view("n_sq", [P, 4, TOK], at_m, end_m)
    wg, _ = sb("wg", [2 * GATE_RANK, 2, H_C * DK_C])
    rd8, _ = sb("rd8", [P, 2 * H_D])
    lg12, _ = sb("lg12", [P, 12])
    deck, _ = sb("deck", [P, 2, H_D])
    etr_r, _ = sb("etr_r", [P, 4])
    assert SB0 + top[0] <= nc.sbuf_usable_end, SB0 + top[0]

    g_in = sem("g_in")
    g_in2, r_in = sem("g_in2"), sem("r_in")
    g_lr, g_lro = sem("g_lr"), sem("g_lro")
    g_x, g_xo = sem("g_x"), sem("g_xo")
    g_ls, g_b = sem("g_ls"), sem("g_b")
    g_e = sem("g_e")
    g_qk = sem("g_qk")
    g_rot, g_roped = sem("g_rot"), sem("g_roped")
    g_t = sem("g_t")
    g_to = [sem("g_to_act"), sem("g_to_dve")]
    g_kv, g_state = sem("g_kv"), sem("g_state")
    g_ctx = sem("g_ctx")
    g_a, g_am = sem("g_a"), sem("g_am")
    g_o, g_oo = sem("g_o"), sem("g_oo")
    r_l2, r_l3 = sem("r_l2"), sem("r_l3")
    r_e, r_m = sem("r_e"), sem("r_m")
    n_in, n_mm, n_ln = sem("n_in"), sem("n_mm"), sem("n_ln")

    n_rt_ok = sem("n_rt_ok")
    r_c, r_cm = sem("r_c"), sem("r_cm")
    wg_zero, odd_in = sem("wg_zero"), sem("odd_in")
    one, _ = sb("one", [P, 1])

    def place(h):
        return h % 2 * 2 + h // 2

    def odd_constants_load(sp):
        rd = a["ret_decay"].rearrange("n d h -> n (d h)")
        sp.dma_start(rd8[:], rd.to_broadcast([P, 2 * H_D])).then_inc(odd_in, 16)
        sp.wait_ge(wg_zero, 1)
        for d in range(2):
            sp.dma_start(wg[GATE_RANK * d:GATE_RANK * (d + 1), d], a["gla_w_gate"][0, d]).then_inc(odd_in, 16)

    def odd_load(sp, load_unit):
        w = a["odd_w_in"].rearrange("n (k p) c -> p (n k) c", p=P)

        def part(n, c, width):
            load_unit(n, n % 2, raw[:, n % 2, 0:DT * width].rearrange("p (k c) -> p k c", c=width), w[:, :, c:c + width])
        part(OB, GLR_COLUMN, P)
        for u, c in enumerate(ODD_T + ODD_TOK):
            if u == 11:
                sp.wait_ge(g_roped, 4)
                sp.dma_start(dist[:], a["odd_constants"][:, 2:6]).then_inc(g_in2, 16)
            part(OB + 1 + u, c, PAIR)
            if u == 1:
                input_split(sp, norm_of["odd"])
                sp.wait_ge(mred_ok, mods_at["odd"])
                sp.dma_start(tab_r[:], a["rope_tables"][2]).then_inc(g_in, 16)
                sp.dma_start(masks[:], a["odd_constants"][:, 0:2]).then_inc(g_in, 16)
                sp.dma_start(restart[:], a["chunk_restart"].to_broadcast([P, TOK])).then_inc(g_in, 16)
        out_load(sp, load_unit, "odd_w_out", OB + 1 + OT + OK, 0, 1)
        sp.wait_ge(tok_mm, proj_n["odd"][1] + 5 * OK)
        sp.dma_start(sr_g[:], a["state_gla"].rearrange("b n d (p two) k v -> (two k) (b n d) p v", two=2)).then_inc(g_in, 16)
        sp.wait_ge(g_ctx, 1)
        sp.dma_start(a["new_state_gla"].rearrange("b n d (p two) k v -> (two k) (b n d) p v", two=2), st_g[:]).then_inc(stored, 16)
        sp.wait_ge(g_kv, N_CHUNK)
        sp.dma_start(sr_r[:], a["state_ret"].rearrange("b n d (p two) k v -> (two k) (b n d) p v", two=2)).then_inc(r_in, 16)
        sp.wait_ge(g_ctx, 2)
        sp.dma_start(a["new_state_ret"].rearrange("b n d (p two) k v -> (two k) (b n d) p v", two=2), st_r[:]).then_inc(stored, 16)
        out_load(sp, load_unit, "odd_w_out", OB + 1 + OT + OK, 1)

    ODD_HEADS = tuple(range(GR, GR + 4)) + tuple(range(RR, RR + 4))

    def odd_pool(pool, st, split_lo):
        n = OB + 2
        for u in range(1 + OT + OK):
            split_lo(n, n % 2)
            n += 1
        for k in range(DT):
            if k == 4:
                pool.wait_ge(stored, 16 * n_mixer_stores)
            pool.wait_ge(o_hi, proj_n["odd"][2] + k + 1)
            nc.gpsimd.tensor_tensor(hl[:, k], feat[:, ODD_HEADS[k]], hh[:, k].bitcast(F32), ALU.subtract).then_inc(o_lo, 1)
        out_pool(pool, split_lo, "odd", n - 2)

    CHUNKS = (LAT,) + tuple(range(LAT))

    def odd_act(act, st, split, res_squares):
        copy = nc.scalar.copy
        n = OB + 2
        p0, t0 = proj_n["odd"][0], proj_n["odd"][1]
        act.wait_ge(g_lr, 1)
        for (lo, hi), ps in runs_alone(psU):
            ins = copy(glr[:, lo:hi], ps[0:2 * GATE_RANK])
        ins.then_inc(g_lro, 1)
        split(n)
        n += 1
        for u in range(OT):
            turned_out(act, copy, 0, feat[:, 2 * u], p0 + u)
            act.wait_ge(proj_mm[1], p0 + u + 1)
            split(n)
            n += 1
            if u == 3:
                act.wait_ge(g_xo, 4)
                st.link(nc.scalar.activation(lt[:], g4[:], ACT.Abs))
                st.link(nc.scalar.activation(lt[:], lt[:], ACT.Exp, scale=-1.0))
                nc.scalar.activation(lt[:], lt[:], ACT.Ln, bias=one[:]).then_inc(g_ls, 1)
                act.wait_ge(odd_in, 3 * 16)
                nc.scalar.activation(lg12[:, 0:8], rd8[:], ACT.Exp, scale=-math.log(2.0))
                for two in range(2):
                    rows = slice(64 * two, 64 * two + 64)
                    ins = nc.scalar.activation(lg12[rows, 8:12], rd8[rows, two:8:2], ACT.Exp, scale=-math.log(2.0))
                st.link(ins)
                st.link(nc.scalar.activation(lg12[:], lg12[:], ACT.Ln, scale=-1.0, bias=one[:]))
                st.mark(nc.scalar.activation(etr_r[:], lg12[:, 8:12], ACT.Exp, scale=float(CHUNK)))
            if u == 6:
                act.wait_ge(g_b, 1)
                nc.scalar.activation(eref[:], refv[:], ACT.Exp)
                nc.scalar.activation(etot[:], totv[:], ACT.Exp)
                nc.scalar.activation(etr[:], etr[:], ACT.Exp).then_inc(r_l3, 1)
                nc.scalar.activation(lt[:, 2:4], lt[:, 0:2], ACT.Exp, scale=-1.0)
                nc.scalar.activation(g4[:, 0:2], g4[:, 2:4], ACT.Exp, scale=-1.0).then_inc(g_e, 1)
                act.wait_ge(g_e, 1)
                nc.scalar.activation(lt[:, 0:2], lt[:, 0:2], ACT.Exp)
                nc.scalar.activation(g4[:, 2:4], g4[:, 2:4], ACT.Exp).then_inc(g_e, 1)
        for u in range(OK):
            for j in range(5):
                c = 5 * u + j
                if c % 2 == 0:
                    tok_out(act, copy, (gv, rv)[u // 2][:, j, u % 2 * PAIR:(u % 2 + 1) * PAIR], t0 + c)
            act.wait_ge(tok_mm, t0 + 5 * (u + 1))
            split(n)
            n += 1
            if u < 2:
                gates = feat[:, (GR, RR)[u]:(GR, RR)[u] + 4]
                act.wait_ge(proj_ok[0], p0 + 4 * (u + 1))
                act.wait_ge(proj_ok[1], p0 + 4 * (u + 1))
                nc.scalar.activation(gates, gates, ACT.Silu)
        for g in range(2 * N_CHUNK):
            if g % 2 == 0:
                act.wait_ge(g_t, g + 1)
                copy(kst_g[:, g // 5, g % 5], banks[g % 5][:, g // 5 * 256:(g // 5 + 1) * 256]).then_inc(g_to[0], 1)
        act.wait_ge(g_in2, 16)
        for d in range(2):
            for p in range(2):
                nc.scalar.activation(decq[:, d, p], dist[:, d], ACT.Exp, scale=lg12[:, 8 + 2 * d + p:9 + 2 * d + p])
        nc.scalar.activation(deck[:, 0], lg12[:, 0:4], ACT.Exp, scale=dist[:, 2, CHUNK - 1:CHUNK])
        nc.scalar.activation(deck[:, 1], lg12[:, 4:8], ACT.Exp, scale=dist[:, 3, 0:1]).then_inc(r_l2, 1)
        act.wait_ge(g_roped, 4)
        for d in range(2):
            if d:
                act.wait_ge(r_m, 1)
            for h in range(H_D):
                ins = nc.scalar.activation(ssum[:, place(h) * CHUNK:(place(h) + 1) * CHUNK], dist[:, 2 + d], ACT.Exp,
                                           scale=lg12[:, 4 * d + h:4 * d + h + 1])
            ins.then_inc(r_e, 1)
        def head_hi(k):
            act.wait_ge(o_ok, proj_n["odd"][2] + k + 1)
            copy(hh[:, k], feat[:, ODD_HEADS[k]]).then_inc(o_hi, 1)

        for kind in range(2):
            for i, c in enumerate(CHUNKS):
                act.wait_ge(g_o, 5 * kind + i + 1)
                first = (GQ, RQ)[kind]
                for odd in range(2):
                    ins = copy(feat[:, first + odd:first + odd + 3:2, c * CHUNK:(c + 1) * CHUNK],
                               psU[:, 2 - odd, 0:2 * CHUNK].rearrange("p (e t) -> p e t", e=2))
                ins.then_inc(g_oo, 1)
            first = (GQ, RQ)[kind]
            if kind == 0:
                act.wait_ge(g_oo, 5)
            else:
                for k in range(H_C):
                    head_hi(k)
            for q in range(2):
                if kind:
                    act.wait_ge(r_c, q + 1)
                nc.scalar.activation(n_sq[:, 2 * q:2 * q + 2], feat[:, first + 2 * q:first + 2 * q + 2],
                                     ACT.Square).then_inc(n_in, 1)
            for q in range(2):
                done = 2 * kind + q + 1
                act.wait_ge(n_mm, done)
                for e in range(2):
                    nc.scalar.activation(n_sq[:, 2 * q + e, 0:512], banks[2 * q + e], ACT.Ln, bias=eps[:], scale=D / DV_C)
                nc.scalar.activation(n_sq[:, 2 * q:2 * q + 2, 512:TOK],
                                     banks[4 + q][:, 0:2 * P].rearrange("p (e t) -> p e t", e=2),
                                     ACT.Ln, bias=eps[:], scale=D / DV_C).then_inc(n_ln, 1)
                act.wait_ge(n_ln, done)
                both = n_sq[:, 2 * q:2 * q + 2]
                nc.scalar.activation(both, both, ACT.Exp, scale=-0.5).then_inc(n_rt_ok, 1)
        for k in range(H_C, DT):
            head_hi(k)
        out_act(act, split, res_squares, "odd", n - 2)

    def odd_dve(dve, st, residual, add_squares, gate_of):
        copy = nc.vector.tensor_copy
        p0, t0 = proj_n["odd"][0], proj_n["odd"][1]

        def chunks(t):
            return t.rearrange("p a (c s) -> p (a c) s", s=CHUNK)

        def roped(count, tile):
            dve.wait_ge(g_rot, count + 1)
            st.link(nc.vector.tensor_tensor(rope, (psA, psB)[count % 2][:, 0:T_LAT], tab_r[:, 1], ALU.mult))
            st.link(nc.vector.tensor_tensor(tile, tile, tab_r[:, 0], ALU.mult))
            nc.vector.tensor_tensor(tile, tile, rope, ALU.add).then_inc(g_roped, 1)
            dve.wait_ge(g_roped, count + 1)

        input_split(dve, norm_of["odd"])
        for u in range(OT):
            turned_out(dve, copy, 1, feat[:, 2 * u + 1], p0 + u)
            if u < 4:
                dve.wait_ge(g_x, u + 1)
                b = ROWS["gla_b_gate"][0] + u
                nc.vector.tensor_scalar(g4[:, u, 0:384], psA[:, 0:384], vec[:, b:b + 1], None, ALU.add)
                nc.vector.tensor_scalar(g4[:, u, 384:TOK], psB[:, 0:256], vec[:, b:b + 1], None, ALU.add).then_inc(g_xo, 1)
            if u == 4:
                dve.wait_ge(g_ls, 1)
                dve.wait_ge(g_xo, 4)
                dve.wait_ge(g_in, 3 * 16)
                st.link(nc.vector.tensor_scalar(g4[:], g4[:], 0.0, 1.0 / GATE_TAU, ALU.min, ALU.mult))
                st.link(nc.vector.scalar_tensor_tensor(out=flat(g4[:]),
                                                       in0=flat(lt[:]), scalar=-1.0 / GATE_TAU,
                                                       in1=flat(g4[:]), op0=ALU.mult, op1=ALU.add))
            if u == 5:
                for t in range(4):
                    st.mark(nc.vector.tensor_tensor_scan(lt[:, t], restart[:], g4[:, t], 0.0, ALU.mult, ALU.add))
                st.wait()
                fwd, bwd, pre = chunks(lt[:, 0:2]), chunks(g4[:, 2:4]), chunks(lt[:, 2:4])
                st.link(nc.vector.tensor_tensor(bwd, bwd, pre, ALU.subtract))
                st.link(nc.vector.tensor_tensor(bwd, bwd, pre[:, :, CHUNK - 1:CHUNK].to_broadcast([P, 10, CHUNK]), ALU.add))
                mid = CHUNK // 2
                for t, (src, end) in enumerate(((fwd, CHUNK - 1), (bwd, 0))):
                    copy(flat(refv[:, 2 * t:2 * t + 2]), src[:, :, mid:mid + 1].rearrange("p a o -> p (a o)"))
                    st.mark(copy(flat(totv[:, 2 * t:2 * t + 2]), src[:, :, end:end + 1].rearrange("p a o -> p (a o)")))
                st.wait()
                for t, src in enumerate((fwd, bwd)):
                    r10 = flat(refv[:, 2 * t:2 * t + 2]).rearrange("p (a o) -> p a o", o=1)
                    st.mark(nc.vector.tensor_tensor(src, src, r10.to_broadcast([P, 10, CHUNK]), ALU.subtract))
                st.mark(nc.vector.tensor_tensor(etr[:], totv[:], refv[:], ALU.subtract))
                st.wait()
                for src in (lt[:, 0:2], g4[:, 2:4]):
                    ins = nc.vector.tensor_scalar(src, src, 43.0, -43.0, ALU.min, ALU.max)
                ins.then_inc(g_b, 1)
            if u in (6, 7):
                for t in range(2):
                    c = 2 * (u - 6) + t
                    roped(c, feat[:, RQ + c, 0:T_LAT])
        scale = float(DK_C) ** -0.5
        dve.wait_ge(g_e, 2)
        dve.wait_ge(proj_ok[0], p0 + 2)
        dve.wait_ge(proj_ok[1], p0 + 2)
        q2, k2 = flat(feat[:, GQ:GQ + 2]), flat(feat[:, GK:GK + 2])
        nc.vector.scalar_tensor_tensor(out=flat(lt[:, 0:2]), in0=q2, scalar=scale, in1=flat(lt[:, 0:2]), op0=ALU.mult, op1=ALU.mult)
        nc.vector.scalar_tensor_tensor(out=flat(g4[:, 2:4]), in0=q2, scalar=scale, in1=flat(g4[:, 2:4]), op0=ALU.mult, op1=ALU.mult)
        nc.vector.tensor_tensor(flat(lt[:, 2:4]), k2, flat(lt[:, 2:4]), ALU.mult)
        nc.vector.tensor_tensor(flat(g4[:, 0:2]), k2, flat(g4[:, 0:2]), ALU.mult).then_inc(g_qk, 1)
        for u in range(OK):
            for j in range(5):
                c = 5 * u + j
                if c % 2 == 1:
                    tok_out(dve, copy, (gv, rv)[u // 2][:, j, u % 2 * PAIR:(u % 2 + 1) * PAIR], t0 + c)
        for g in range(2 * N_CHUNK):
            if g % 2 == 1:
                dve.wait_ge(g_t, g + 1)
                copy(kst_g[:, g // 5, g % 5], banks[g % 5][:, g // 5 * 256:(g // 5 + 1) * 256]).then_inc(g_to[1], 1)
        s3 = ssum[:, 0:4 * CHUNK].rearrange("p (h t) -> p h t", h=4)
        for d in range(2):
            m = masks[:, d:d + 1, :].to_broadcast([P, 4, CHUNK])
            dve.wait_ge(r_e, d + 1)
            if d == 0:
                nc.vector.tensor_tensor(mret[:], s3, m, ALU.mult).then_inc(r_m, 1)
            else:
                dve.wait_ge(r_m, 1)
                st.link(nc.vector.tensor_tensor(s3, s3, m, ALU.mult))
                st.link(nc.vector.tensor_tensor(mret[:], mret[:], s3, ALU.add))
                st.mark(nc.vector.tensor_scalar(mret[:], mret[:], float(DK_D) ** -0.5, None, ALU.mult))
        dve.wait_ge(r_l2, 1)
        st.link(nc.vector.tensor_scalar(deck[:], deck[:], float(DK_D) ** -0.5, None, ALU.mult))

        def kv_of(d, c):
            return banks[c][:, d * 256:(d + 1) * 256].rearrange("p (a v) -> p a v", a=2)

        def state_chain(kind, ss, sr, final, masked):
            def per(v):
                return v.to_broadcast([P, 2, DV_C])

            def at_mid(d, c):
                return per(eref[:, 2 * d:2 * d + 2, c:c + 1])

            def over(d, c):
                return per(etot[:, 2 * d:2 * d + 2, c:c + 1]) if kind == 0 else \
                    per(etr_r[:, 2 * d:2 * d + 2].rearrange("p (a o) -> p a o", o=1))

            def tail(d, c):
                return per(etr[:, 2 * d:2 * d + 2, c:c + 1])
            for d in range(2):
                if kind == 0:
                    ins = nc.vector.tensor_tensor(final[:, d], kv_of(d, LAT), tail(d, LAT), ALU.mult)
                else:
                    ins = copy(final[:, d], kv_of(d, LAT))
            ins.then_inc(g_ctx, 1)
            masked(0)
            for i in range(LAT):
                pairs = ((0, i), (1, LAT - 1 - i))
                for d, c in pairs:
                    if kind == 0:
                        ins = nc.vector.tensor_tensor(ss[:, d, c], sr[:, d], at_mid(d, c), ALU.mult)
                    else:
                        ins = copy(ss[:, d, c], sr[:, d])
                if i == LAT - 1:
                    ins.then_inc(g_state, 1)
                    break
                st.link(ins)
                for d, c in pairs:
                    st.mark(nc.vector.tensor_tensor(sr[:, d], sr[:, d], over(d, c), ALU.mult))
                    if kind == 0:
                        st.mark(nc.vector.tensor_tensor(kvt(d), kv_of(d, c), tail(d, c), ALU.mult))
                st.wait()
                for d, c in pairs:
                    st.mark(nc.vector.tensor_tensor(sr[:, d], sr[:, d], kvt(d) if kind == 0 else kv_of(d, c), ALU.add))
                st.wait()
            for i in range(1, 5):
                masked(i)
                if kind:
                    finish_head(dve, st, 0, i - 1)

        def kvt(d):
            return ssum[:, d * 256:(d + 1) * 256].rearrange("p (a v) -> p a v", a=2)

        def masked_g(i):
            dve.wait_ge(g_a, i + 1)
            if i >= 2:
                dve.wait_ge(g_o, i - 1)
            f = am[:, i % 2]
            both = masks[:].rearrange("p d (o t) -> p d o t", o=1).to_broadcast([P, 2, 2, CHUNK])
            for half, bank in enumerate((psA, psB)):
                st.mark(nc.vector.tensor_tensor(am2[:, half], bank[:, :].rearrange("p (d e t) -> p d e t", d=2, e=2),
                                                both, ALU.mult))
            st.wait()
            nc.vector.tensor_tensor(f.rearrange("p (o e) t -> p o e t", o=2), am2[:, :, 0], am2[:, :, 1], ALU.add).then_inc(g_am, 1)
            dve.wait_ge(g_am, i + 1)

        def masked_r(i):
            dve.wait_ge(g_a, 5 + i + 1)
            if i >= 1:
                dve.wait_ge(g_o, 5 + i - 1)
            for half, bank in enumerate((psA, psB)):
                e = slice(2 * half, 2 * half + 2)
                ins = nc.vector.tensor_tensor(am[:, i % 2, e], bank[:, 0:2 * CHUNK].rearrange("p (e t) -> p e t", e=2),
                                              mret[:, e], ALU.mult)
            ins.then_inc(g_am, 1)

        dve.wait_ge(r_l3, 1)
        dve.wait_ge(g_in, 4 * 16)
        dve.wait_ge(g_kv, N_CHUNK)
        state_chain(0, ss_g, sr_g, st_g, masked_g)
        for c in range(N_CHUNK):
            dve.wait_ge(g_t, 2 * N_CHUNK + c + 1)
            for d in range(2):
                ins = nc.vector.tensor_tensor(kst_r[:, d, c].rearrange("p (h k) -> p h k", h=4),
                                              banks[c][:, 0:256].rearrange("p (h k) -> p h k", h=4),
                                              deck[:, d].rearrange("p (h o) -> p h o", o=1).to_broadcast([P, 4, DK_D]),
                                              ALU.mult)
            ins.then_inc(g_to[1], 1)
        dve.wait_ge(g_o, 5)
        for d in range(2):
            for p in range(2):
                ins = nc.vector.tensor_tensor(qret[:, d, p].rearrange("p (c t) -> p c t", t=CHUNK),
                                              feat[:, RQ + p, 0:T_LAT].rearrange("p (c t) -> p c t", t=CHUNK),
                                              decq[:, d, p:p + 1, :].to_broadcast([P, LAT, CHUNK]), ALU.mult)
        ins.then_inc(g_qk, 1)
        dve.wait_ge(r_in, 16)
        dve.wait_ge(g_kv, 2 * N_CHUNK)
        state_chain(1, ss_r, sr_r, st_r, masked_r)
        for q in range(2):
            centre(dve, q)
        for h in range(H_D):
            finish_head(dve, st, 1, h)
        dve.wait_ge(o_ok, proj_n["odd"][2] + 8)
        out_dve(dve, st, residual, add_squares, gate_of, "odd", 1)

    def centre(dve, q):
        dve.wait_ge(r_cm, q + 1)
        for e in range(2):
            t = feat[:, RQ + 2 * q + e, 0:512]
            nc.vector.scalar_tensor_tensor(out=t, in0=banks[2 * q + e], scalar=-float(D) / DV_D, in1=t,
                                           op0=ALU.mult, op1=ALU.add)
        t = feat[:, RQ + 2 * q:RQ + 2 * q + 2, 512:TOK]
        nc.vector.scalar_tensor_tensor(out=t, in0=banks[4 + q][:, 0:2 * P].rearrange("p (e t) -> p e t", e=2),
                                       scalar=-float(D) / DV_D, in1=t, op0=ALU.mult, op1=ALU.add).then_inc(r_c, 1)

    def finish_head(dve, st, kind, h):
        first, gate, gain = ((GQ, GR, ROWS["gla_norm"][0]), (RQ, RR, ROWS["ret_norm"][0]))[kind]
        dve.wait_ge(n_rt_ok, 2 * kind + h // 2 + 1)
        t = feat[:, first + h]
        st.link(nc.vector.scalar_tensor_tensor(out=t, in0=t, scalar=vec[:, gain:gain + 1], in1=n_sq[:, h],
                                               op0=ALU.mult, op1=ALU.mult))
        nc.vector.tensor_tensor(feat[:, gate + h], t, feat[:, gate + h], ALU.mult).then_inc(o_ok, 1)

    def odd_pe(pe, part_products, unit_tile, norm_sum):
        r = norm_of["odd"]
        p0, t0 = proj_n["odd"][0], proj_n["odd"][1]

        def turn(out, in_):
            return nc.tensor.transpose(out, in_, ident[:])

        def rotate(count, tile):
            if count < 2:
                pe.wait_ge(g_xo, 4)
            else:
                pe.wait_ge(g_roped, count - 1)
            pe.wait_ge(proj_ok[count % 2], p0 + (RQ + count) // 2 + 1)
            nc.tensor.matmul((psA, psB)[count % 2][:, 0:T_LAT], rot[:, 2, :], tile, start=True, stop=True).then_inc(g_rot, 1)

        pe.wait_ge(w_lo, OB + 1)
        slot = OB % 2
        for k in range(DT):
            input_split(pe, r, k)
            w = slice(k * P, (k + 1) * P)
            ins = part_products(wh[:, slot, w], wl[:, slot, w], hh[:, k], hl[:, k], runs_alone(psU), k == 0, k == DT - 1)
        ins.then_inc(g_lr, 1)
        for u in range(OT):
            turned_unit_pe(pe, unit_tile, OB + 1 + u, p0 + u, r, second_bank=None if u else g_lro)
            if u < 4:
                if u:
                    pe.wait_ge(g_xo, u)
                else:
                    pe.wait_ge(odd_in, 3 * 16)
                w = wg[:, u // 2, u % 2 * P:(u % 2 + 1) * P]
                nc.tensor.matmul(psA[:, 0:384], w, glr[:, 0:384], start=True, stop=True)
                nc.tensor.matmul(psB[:, 0:256], w, glr[:, 384:TOK], start=True, stop=True).then_inc(g_x, 1)
            if u in (6, 7):
                for t in range(2):
                    c = 2 * (u - 6) + t
                    rotate(c, feat[:, RQ + c, 0:T_LAT])
        with pe.Fori(0, OK // 2) as i:
            for s in range(2):
                tok_unit_pe(pe, OB + 1 + OT + s, t0 + 5 * s, i)
        pe.wait_ge(g_qk, 1)
        for b in range(2):
            pe.wait_ge(proj_ok[b], p0 + OT)
            pe.wait_ge(tok_ok[b], (t0 + 5 * OK) // 2)
        for g in range(2 * N_CHUNK):
            d, c = g // N_CHUNK, g % N_CHUNK
            if d:
                pe.wait_ge(g_to[c % 2], c // 2 + 1)
            for p in range(2):
                src = lt[:, 2 + p] if d == 0 else g4[:, p]
                ins = turn(banks[c][:, d * 256 + p * P:d * 256 + (p + 1) * P], src[:, c * CHUNK:(c + 1) * CHUNK])
            ins.then_inc(g_t, 1)

        def keys_values(kst, v):
            for c in range(N_CHUNK):
                for d in range(2):
                    for h in range(4):
                        rows = slice(64 * (h % 2), 64 * (h % 2) + 64)
                        col = d * 256 + h // 2 * P
                        ins = nc.tensor.matmul(banks[c][rows, col:col + P], kst[:, d, c, h * 64:(h + 1) * 64],
                                               v[:, c, h * P:(h + 1) * P], start=True, stop=True)
                ins.then_inc(g_kv, 1)

        for b in range(2):
            pe.wait_ge(g_to[b], N_CHUNK)
        keys_values(kst_g, gv)

        def products(kind, i):
            c = CHUNKS[i]
            cols = slice(c * CHUNK, (c + 1) * CHUNK)
            n = 5 * kind + i
            if n:
                pe.wait_ge(g_am, n)
            for h in range(4):
                rows = slice(64 * (h % 2), 64 * (h % 2) + 64)
                bank, at = (psA, psB)[h % 2], h // 2 * CHUNK
                out, out2 = bank[:, at:at + CHUNK], bank[:, 2 * CHUNK + at:3 * CHUNK + at]
                if kind == 0:
                    nc.tensor.matmul(out, lt[rows, 2 + h // 2, cols], lt[rows, h // 2, cols], start=True, stop=True)
                    ins = nc.tensor.matmul(out2, g4[rows, h // 2, cols], g4[rows, 2 + h // 2, cols], start=True, stop=True)
                else:
                    ins = nc.tensor.matmul(out, feat[rows, RK + h // 2, cols], feat[rows, RQ + h // 2, cols],
                                           start=True, stop=True)
            ins.then_inc(g_a, 1)

        def outputs(kind, i):
            c = CHUNKS[i]
            cols = slice(c * CHUNK, (c + 1) * CHUNK)
            n = 5 * kind + i
            pe.wait_ge(g_am, n + 1)
            if n:
                pe.wait_ge(g_oo, n)
            if i == 0:
                pe.wait_ge(g_ctx, kind + 1)
            if i == 1:
                pe.wait_ge(g_state, kind + 1)
            v, ss = ((gv, ss_g), (rv, ss_r))[kind]
            for h in range(4):
                rows = slice(64 * (h % 2), 64 * (h % 2) + 64)
                out = psU[:, 2 - h % 2, h // 2 * CHUNK:(h // 2 + 1) * CHUNK]
                ins = nc.tensor.matmul(out, v[:, c, h * P:(h + 1) * P], am[:, i % 2, place(h)], start=True, stop=c == LAT)
                if c < LAT:
                    for d in range(2):
                        q = (lt[rows, h // 2, cols], g4[rows, 2 + h // 2, cols])[d] if kind == 0 else qret[rows, d, h // 2, cols]
                        ins = nc.tensor.matmul(out, ss[rows, d, c, h // 2], q, start=False, stop=d == 1)
            ins.then_inc(g_o, 1)

        products(0, 0)
        for i in range(5):
            if i + 1 < 5:
                products(0, i + 1)
            outputs(0, i)
        def means(src, q, signal):
            for e in range(2):
                nc.tensor.matmul(banks[2 * q + e], ones[:], src[:, 2 * q + e, 0:512], start=True, stop=True)
                ins = nc.tensor.matmul(banks[4 + q][:, e * P:(e + 1) * P], ones[:], src[:, 2 * q + e, 512:TOK],
                                       start=True, stop=True)
            ins.then_inc(signal, 1)

        for q in range(2):
            pe.wait_ge(n_in, q + 1)
            means(n_sq, q, n_mm)
        products(1, 0)
        pe.wait_ge(n_ln, 2)
        pe.wait_ge(g_roped, 4)
        for c in range(N_CHUNK):
            for p in range(2):
                ins = turn(banks[c][:, p * P:(p + 1) * P], feat[:, RK + p, c * CHUNK:(c + 1) * CHUNK])
            ins.then_inc(g_t, 1)
        pe.wait_ge(g_to[1], 2 * N_CHUNK)
        keys_values(kst_r, rv)
        for i in range(5):
            if i + 1 < 5:
                products(1, i + 1)
            outputs(1, i)
        pe.wait_ge(g_oo, 10)
        for q in range(2):
            means(feat[:, RQ:RQ + H_D], q, r_cm)
        for q in range(2):
            pe.wait_ge(n_in, 2 + q + 1)
            means(n_sq, q, n_mm)
        pe.wait_ge(n_ln, 4)
        out_pe(pe, unit_tile, "odd", OB + 1 + OT + OK)

    block = ctx.enter_context(nc.Block())

    @block.sync
    def _(sp):
        def load_unit(n, slot, dst, src):
            if not isinstance(n, int) or n >= 2:
                sp.wait_ge(w_hi, n - 1)
                sp.wait_ge(w_lo, n - 1)
            sp.dma_start(dst, src).then_inc(raw_in[slot], 16)

        def load_mod(q, slot, src):
            if not isinstance(q, int) or q >= MOD_HEAD + 2:
                sp.wait_ge(macc_ok, q - 1)
            sp.dma_start(mraw[:, slot], src).then_inc(mod_in[slot], 16)

        mod_w = a["mod_w"].rearrange("l (k p) c -> p k l c", p=P)

        def mod_src_run(layer, first, step):
            return mod_w[:, :, layer, bass.ds(first * PAIR + step, PAIR)]

        for name in ROWS:
            r0, n = ROWS[name]
            src = a[name]
            if name == "norm_g":
                src = src.rearrange("l j (t p) -> (l j t) p", p=P)
            elif name == "gla_b_gate":
                src = src.rearrange("n d (t p) -> (n d t) p", p=P)
            elif len(src.shape) == 1:
                src = src.rearrange("(t p) -> t p", p=P)
            else:
                src = src.rearrange("n (t p) -> (n t) p", p=P)
            sp.dma_start(rows[r0:r0 + n, :], src).then_inc(start_in, 16)
        mb = a["mod_b"].rearrange("l (t p) -> (l t) p", p=P)
        sp.dma_start(brows[:, 0, :], mb[0:P, :]).then_inc(start_in, 16)
        sp.dma_start(brows[0:MOD_ROWS - P, 1, :], mb[P:MOD_ROWS, :]).then_inc(start_in, 16)
        sp.dma_start(rot[:], a["rope_rotations"]).then_inc(start_in, 16)
        sp.dma_start(mshift[:], mod_w[:, :, 0, 0:D]).then_inc(head_in[0], 16)
        sp.dma_start(mscale[:], mod_w[:, :, 0, D:2 * D]).then_inc(head_in[1], 16)

        def ffn_src(f, part, i, s):
            if part in (0, 2):
                w = a["ffn_w_gate" if s == 0 else "ffn_w_up"].rearrange("l j (k p) c -> p k (l j) c", p=P)
                first = 0 if part == 0 else FIRST_PAIRS * PAIR
                return w[:, :, f, bass.ds(i * PAIR + first, PAIR)]
            w = a["ffn_w_down"].rearrange("l j (k p) c -> p k (l j) c", p=P)
            kt = HALF_TILES[part // 2] // 2
            k0 = (HALF_TILES[0] if part == 3 else 0) + s * kt
            return w[:, k0:k0 + kt, f, bass.ds(i * PAIR, PAIR)]

        def ffn_load(f):
            for part, base, count, _ in ffn_parts(f):
                mods, q0 = MOD_PLAN[f][part], MOD_BASE[f, part]
                cuts = sorted({0, count, min(count, mods // 2), *([(36 - q0) // 2] if q0 < 36 < q0 + mods else [])})
                for lo, hi in zip(cuts, cuts[1:]):
                    def load(i):
                        for s in range(2):
                            slot = (base + s) % 2
                            kt = DT if part in (0, 2) else HALF_TILES[part // 2] // 2
                            dst = raw[:, slot, 0:kt * PAIR].rearrange("p (k c) -> p k c", c=PAIR)
                            load_unit(i * 2 + (base + s), slot, dst, ffn_src(f, part, i, s))
                        for s in range(2):
                            if 2 * lo < mods:
                                q = q0 + s
                                layer = 0 if q0 + 2 * lo < 36 else 1
                                load_mod(i * 2 + q, q % 2, mod_src_run(layer, q - 36 * layer, i * 2 * PAIR))
                    turns(sp, lo, hi, load, apart=base == 0 and lo == 0)

        for name in phases:
            if name.startswith("ffn"):
                ffn_load(int(name[3]))
                if name == phases[0]:
                    odd_constants_load(sp)
            elif name == "even":
                even_load(sp, load_unit)
            else:
                odd_load(sp, load_unit)
        for j in range(TOK // P):
            sp.wait_ge(turn_dve, 3 + 5 + j + 1)
            sp.wait_ge(turn_act, 5 + j + 1)
            dst = a["y_sample"][0, j * P:(j + 1) * P] if j < T_LAT // P else a["y_prompt"][0]
            sp.dma_start(dst, yout[:, j, :]).then_inc(stored, 16)
        sp.wait_ge(stored, 16 * (TOK // P + n_mixer_stores))

    @block.gpsimd
    def _(pool):
        st = Steps(pool, pool_steps)
        nc.gpsimd.memset(wg[:], 0.0).then_inc(wg_zero, 1)
        st.mark(nc.gpsimd.memset(ident[:], 0.0))
        nc.gpsimd.memset(ones[:], 1.0 / D).then_inc(const_ok, 1)
        nc.gpsimd.memset(eps[:], EPS).then_inc(const_ok, 1)
        st.wait()
        nc.gpsimd.affine_select(out=ident[:], in_=ident[:], compare_op=ALU.not_equal, fill=1.0, base=0,
                                pattern=[[-1, P]], channel_multiplier=1).then_inc(const_ok, 1)
        nc.gpsimd.memset(one[:], 1.0).then_inc(const_ok, 1)

        def split_lo(n, slot):
            pool.wait_ge(w_hi, n + 1)
            nc.gpsimd.tensor_tensor(wl[:, slot], raw[:, slot], wh[:, slot].bitcast(F32), ALU.subtract).then_inc(w_lo, 1)

        def norm_lo(r):
            for k in range(1, DT, 2):
                pool.wait_ge(h_hi, DT * r + k + 1)
                nc.gpsimd.tensor_tensor(hl[:, k], nf[:, k % 4], hh[:, k].bitcast(F32), ALU.subtract).then_inc(h_lo[1], 1)

        def ffn(f):
            last = f"ffn{f}" == phases[-1]
            for part, base, count, pair0 in ffn_parts(f):
                if part in (0, 2):
                    with pool.Fori(0, count) as i:
                        t = i * 2 + (FT * f + 2 * pair0)
                        split_lo(i * 2 + (base + 2), base % 2)
                        for m in range(2):
                            pool.wait_ge(a_hi, t + (m + 1))
                            nc.gpsimd.tensor_tensor(tile_of(al, i * 2 + m), af[:, m],
                                                    tile_of(ah, i * 2 + m).bitcast(F32), ALU.subtract).then_inc(a_lo, 1)
                            if m == 0:
                                split_lo(i * 2 + (base + 3), (base + 1) % 2)
                else:
                    n = count - 1 if last and part == 3 else count
                    with pool.Fori(0, n) as i:
                        split_lo(i * 2 + (base + 2), base % 2)
                        split_lo(i * 2 + (base + 3), (base + 1) % 2)

        split_lo(0, 0)
        split_lo(1, 1)
        for name in phases:
            norm_lo(norm_of[name])
            if name.startswith("ffn"):
                ffn(int(name[3]))
            elif name == "even":
                even_pool(pool, st, split_lo)
            else:
                odd_pool(pool, st, split_lo)

    @block.scalar
    def _(act):
        st = Steps(act, act_steps)

        def split(n0, i=0):
            slot = n0 % 2
            act.wait_ge(raw_in[slot], (i * 16) + (n0 // 2 * 16 + 16))
            nc.scalar.copy(wh[:, slot], raw[:, slot]).then_inc(w_hi, 1)

        def norm_hi(r, shift_block=0):
            act.wait_ge(ms_ok, r + 1)
            nc.scalar.activation(rstd[:, 0:384], psA[:, 0:384], ACT.Ln, bias=eps[:])
            st.link(nc.scalar.activation(rstd[:, 384:TOK], psB[:, 0:256], ACT.Ln, bias=eps[:]))
            nc.scalar.activation(rstd[:], rstd[:], ACT.Exp, scale=-0.5).then_inc(rms_ok, 1)
            if r == norm_of["final"]:
                return
            for k in range(DT):
                act.wait_ge(hf_ok, DT * r + k + 1)
                out = nf[:, k % 4] if k % 2 else hh[:, k]
                for lo, hi, c in CONDS:
                    ins = nc.scalar.activation(out[:, lo:hi], nf[:, k % 4, lo:hi], ACT.Identity,
                                               bias=mod[:, c, shift_block * DT + k:shift_block * DT + k + 1])
                if k % 2:
                    st.link(ins)
                    ins = nc.scalar.copy(hh[:, k], nf[:, k % 4])
                ins.then_inc(h_hi, 1)

        def res_squares(r, i, m, n_res):
            act.wait_ge(res_ok[m], i + n_res)
            act.wait_ge(ssum_ok, i * 2 + (DT * r + m - 1))
            nc.scalar.activation(sg[:, m], tile_of(x, i * 2 + m), ACT.Square).then_inc(sq_ok, 1)

        def ffn(f):
            last = f"ffn{f}" == phases[-1]
            r = norm_of[f"ffn{f}"]
            for part, base, count, pair0 in ffn_parts(f):
                if part in (0, 2):
                    def pair(i):
                        t = i * 2 + (FT * f + 2 * pair0)
                        passed(act, prod_ok, t)
                        act.wait_ge(gate_mm, t + 2)
                        split(base + 2, i)
                        for m in range(2):
                            for (lo, hi), ps in runs_of(psG, m):
                                ins = nc.scalar.activation(sg[:, m, lo:hi], ps, ACT.Silu)
                            ins.then_inc(silu_ok, 1)
                        for m in range(2):
                            act.wait_ge(prod_ok, t + (m + 1))
                            if m == 1:
                                split(base + 3, i)
                            nc.scalar.copy(tile_of(ah, i * 2 + m), af[:, m]).then_inc(a_hi, 1)
                    turns(act, 0, count, pair, apart=base == 0)
                else:
                    def pair(i, more):
                        if more:
                            act.wait_ge(w_used, i + (used_base[f, part] + 1))
                            split(base + 2, i)
                            act.wait_ge(down_mm[1], i + (res_base[f, part] + 1))
                            split(base + 3, i)
                        if part == 3:
                            for m in range(2):
                                res_squares(r + 1, i, m, res_base[f, part] + 1)
                    cut = last and part == 3
                    with act.Fori(0, count - 1 if cut else count) as i:
                        pair(i, True)
                    if cut:
                        pair(count - 1, False)

        act.dma_start(xin[:, 0:4, :], a["x_sample"].rearrange("b (t p) d -> p (b t) d", p=P)).then_inc(x_in, 16)
        act.dma_start(xin[:, 4, :], a["x_prompt"].rearrange("b p d -> (b p) d")).then_inc(x_in, 16)
        act.wait_ge(turn_dve, 3)
        for c, name in enumerate(("c", "c_ctx")):
            r0, n = ROWS[name]
            nc.scalar.activation(cs[:, :, c], vec[:, r0:r0 + n], ACT.Silu).then_inc(cs_ok, 1)
        for g in range(1, 10, 2):
            j, half = g // 2, g % 2
            act.wait_ge(turn_mm, 3 + g + 1)
            nc.scalar.copy(x[:, 4 * half:4 * half + 4, j * P:(j + 1) * P],
                           banks[g % 6].rearrange("p (k t) -> p k t", k=4)).then_inc(turn_act, 1)
        act.wait_ge(turn_act, 5)
        act.wait_ge(turn_dve, 3 + 5)
        for k in range(DT):
            if k >= 2:
                act.wait_ge(ssum_ok, k - 1)
            nc.scalar.activation(sg[:, k % 2], x[:, k], ACT.Square).then_inc(sq_ok, 1)
        for b in range(2):
            act.wait_ge(head_mm, b + 1)
            nc.scalar.copy(mrow[:, b * D:(b + 1) * D], flat((psG, psU)[b][0:2, 0:2, :])).then_inc(mrow_ok, 1)
        split(0)
        split(1)
        for name in phases:
            norm_hi(norm_of[name], SHIFT_OF[name])
            if name.startswith("ffn"):
                ffn(int(name[3]))
            elif name == "even":
                even_act(act, st, split, res_squares)
            else:
                odd_act(act, st, split, res_squares)
        norm_hi(norm_of["final"])
        for g in range(1, 10, 2):
            act.wait_ge(turn_mm, 13 + g + 1)
            nc.scalar.copy(yout[:, g // 2, g % 2 * 512:(g % 2 + 1) * 512], banks[g % 6]).then_inc(turn_act, 1)

    @block.vector
    def _(dve):
        st = Steps(dve, dve_steps)

        def mod_sum(q0, i=0):
            slot = q0 % 2
            dve.wait_ge(mturn_ok, (i * 2) + (q0 - 1))
            dve.wait_ge(mod_in[slot], (i * 16) + ((q0 - MOD_HEAD) // 2 * 16 + 16))
            for k in range(DT):
                for c in range(2):
                    if k == 0:
                        st.mark(nc.vector.tensor_scalar(macc[:, slot, c], mraw[:, slot, k], cs[:, k, c:c + 1], None, ALU.mult))
                        continue
                    st.wait(back=1)
                    ins = nc.vector.scalar_tensor_tensor(out=macc[:, slot, c], in0=mraw[:, slot, k],
                                                         scalar=cs[:, k, c:c + 1], in1=macc[:, slot, c],
                                                         op0=ALU.mult, op1=ALU.add)
                    if k == DT - 1 and c == 1:
                        ins.then_inc(macc_ok, 1)
                    else:
                        st.mark(ins)

        def mod_reduce(q0, i=0):
            dve.wait_ge(mturn_ok, (i * 2) + (q0 + 1))
            st.link(nc.vector.tensor_reduce(mred[:], psA[:, :].rearrange("p (c t b) -> p c t b", c=2, b=P), AX.X, ALU.add))
            col = bass.ds(i * 4 + 2 * q0, 2)
            nc.vector.tensor_tensor(mod[:, :, col], mred[:],
                                    modb[:, col].rearrange("p (o t) -> p o t", o=1).to_broadcast([P, 2, 2]),
                                    ALU.add).then_inc(mred_ok, 1)

        def norm(r, gain, scale_block, shift_block):
            dve.wait_ge(mred_ok, 4 * (scale_block + 1))
            if r:
                dve.wait_ge(hf_ok, DT * r)
            st.link(nc.vector.scalar_tensor_tensor(
                out=g1[:], in0=modv(scale_block), scalar=1.0,
                in1=vec[:, gain:gain + DT].rearrange("p (o t) -> p o t", o=1).to_broadcast([P, 2, DT]),
                op0=ALU.add, op1=ALU.mult))
            dve.wait_ge(rms_ok, r + 1)
            for k in range(DT):
                if k >= 4:
                    input_split(dve, r, k - 4)
                for lo, hi, c in CONDS:
                    ins = nc.vector.scalar_tensor_tensor(out=nf[:, k % 4, lo:hi], in0=x[:, k, lo:hi], scalar=g1[:, c, k:k + 1],
                                                         in1=rstd[:, lo:hi], op0=ALU.mult, op1=ALU.mult)
                ins.then_inc(hf_ok, 1)
                if k % 2:
                    e = k - 1
                    dve.wait_ge(h_hi, DT * r + e + 1)
                    for lo, hi, c in CONDS:
                        ins = nc.vector.scalar_tensor_tensor(out=hl[:, e, lo:hi], in0=nf[:, e % 4, lo:hi],
                                                             scalar=mod[:, c, shift_block * DT + e:shift_block * DT + e + 1],
                                                             in1=hh[:, e, lo:hi].bitcast(F32), op0=ALU.add, op1=ALU.subtract)
                    ins.then_inc(h_lo[0], 1)

        def modv(b):
            return mod[:, :, b * DT:(b + 1) * DT]

        def residual(i, m, n_before):
            dve.wait_ge(down_mm[m], i + (n_before + 1))
            ps = (psG, psU)[m]
            for lo, hi, c in COND_PIECES:
                src = ps[:, 1, lo:hi] if hi <= 384 else ps[:, 0, lo - 384:hi - 384]
                xt = tile_of(x, i * 2 + m, lo, hi)
                ins = nc.vector.scalar_tensor_tensor(out=xt, in0=src, scalar=hg_of(i * 2 + m, c), in1=xt,
                                                     op0=ALU.mult, op1=ALU.add)
            ins.then_inc(res_ok[m], 1)

        def hg_of(t, c):
            return hgate[:, c, t:t + 1] if isinstance(t, int) else hgate[:, c, bass.ds(t, 1)]

        def add_squares(i, m, r):
            dve.wait_ge(sq_ok, i * 2 + (DT * r + m + 1))
            dve.wait_ge(ssum_ok, i * 2 + (DT * r + m))
            nc.vector.tensor_tensor(ssum[:], ssum[:], sg[:, m], ALU.add).then_inc(ssum_ok, 1)

        def gate_of(block, factor, n_res):
            dve.wait_ge(mred_ok, 4 * (block + 1))
            if n_res:
                dve.wait_ge(res_ok[1], n_res)
            st.link(nc.vector.tensor_scalar(hgate[:], modv(block), factor, None, ALU.mult))

        def ffn(f):
            l, j = f // 2, f % 2
            last = f"ffn{f}" == phases[-1]
            r = norm_of[f"ffn{f}"]
            for part, base, count, pair0 in ffn_parts(f):
                mods, q0 = MOD_PLAN[f][part], MOD_BASE[f, part]
                if part == 1:
                    gate_of(l * N_MOD + (2 if j == 0 else 8), 0.5, res_base[f, 1])
                if part == 3:
                    dve.wait_ge(hf_ok, DT * (r + 1))
                    st.link(nc.vector.memset(ssum[:], 0.0))
                cuts = sorted({0, min(count, mods // 2), count})
                for lo, hi in zip(cuts, cuts[1:]):
                    carries = 2 * lo < mods
                    start = st.n
                    assert not carries or lo == 0

                    def turn(i):
                        if carries:
                            st.n = i * PER_MOD + start
                        if part in (0, 2):
                            t = i * 2 + (FT * f + 2 * pair0)
                            if carries:
                                mod_sum(q0, i)
                                mod_reduce(q0, i)
                                mod_sum(q0 + 1, i)
                            passed(dve, a_lo, t)
                            dve.wait_ge(up_mm, t + 2)
                            for m in range(2):
                                dve.wait_ge(silu_ok, t + (m + 1))
                                for (a0, a1), ps in runs_of(psU, m):
                                    ins = nc.vector.tensor_tensor(af[:, m, a0:a1], sg[:, m, a0:a1], ps, ALU.mult)
                                ins.then_inc(prod_ok, 1)
                            if carries:
                                mod_reduce(q0 + 1, i)
                        else:
                            if carries:
                                mod_sum(q0, i)
                                mod_reduce(q0, i)
                                mod_sum(q0 + 1, i)
                            for m in range(2):
                                residual(i, m, res_base[f, part])
                            if carries:
                                mod_reduce(q0 + 1, i)
                            if part == 3:
                                for m in range(2):
                                    add_squares(i, m, r + 1)
                    turns(dve, lo, hi, turn, apart=base == 0 and lo == 0)
                    st.n = start + hi * PER_MOD if carries else start

        dve.wait_ge(turn_mm, 1)
        nc.vector.tensor_copy(vec[:], psA[:, 0:N_ROWS]).then_inc(turn_dve, 1)
        dve.wait_ge(turn_dve, 1)
        sub_g = vec[:, ROWS["diff_subln"][0]:ROWS["diff_subln"][0] + 1]
        nc.vector.tensor_scalar(sub_g, sub_g, 1.0 - LAM_INIT, None, ALU.mult)
        dve.wait_ge(turn_mm, 3)
        nc.vector.tensor_copy(modb[:, 0:P], psB[:, 0:P]).then_inc(turn_dve, 1)
        nc.vector.tensor_copy(modb[:, P:MOD_ROWS], psB[:, P:MOD_ROWS]).then_inc(turn_dve, 1)
        dve.wait_ge(cs_ok, 2)
        for g in range(0, 10, 2):
            dve.wait_ge(turn_mm, 3 + g + 1)
            nc.vector.tensor_copy(x[:, 0:4, g // 2 * P:(g // 2 + 1) * P],
                                  banks[g % 6].rearrange("p (k t) -> p k t", k=4)).then_inc(turn_dve, 1)
        st.link(nc.vector.memset(ssum[:], 0.0))
        for k in range(DT):
            dve.wait_ge(sq_ok, k + 1)
            if k:
                dve.wait_ge(ssum_ok, k)
            nc.vector.tensor_tensor(ssum[:], ssum[:], sg[:, k % 2], ALU.add).then_inc(ssum_ok, 1)
        dve.wait_ge(mturn_ok, MOD_HEAD)
        for c, counted in enumerate((macc_ok, mred_ok)):
            nc.vector.tensor_tensor(mod[:, c, 0:2 * DT], psA[:, 0:4 * DT].rearrange("p (t c) -> p t c", c=2)[:, :, c],
                                    modb[:, 0:2 * DT], ALU.add).then_inc(counted, MOD_HEAD)
        for name in phases:
            l = {"ffn0": 0, "even": 0, "ffn1": 0}.get(name, 1)
            j = {"ffn0": 0, "ffn2": 0, "even": 1, "odd": 1}.get(name, 2)
            norm(norm_of[name], ROWS["norm_g"][0] + (l * 3 + j) * DT, SHIFT_OF[name] + 1, SHIFT_OF[name])
            if name.startswith("ffn"):
                ffn(int(name[3]))
            elif name == "even":
                even_dve(dve, st, residual, add_squares, gate_of)
            else:
                odd_dve(dve, st, residual, add_squares, gate_of)
        dve.wait_ge(rms_ok, norm_of["final"] + 1)
        for k in range(DT):
            g = ROWS["final_g"][0] + k
            nc.vector.scalar_tensor_tensor(out=x[:, k], in0=x[:, k], scalar=vec[:, g:g + 1], in1=rstd[:],
                                           op0=ALU.mult, op1=ALU.mult).then_inc(hf_ok, 1)
        for g in range(0, 10, 2):
            dve.wait_ge(turn_mm, 13 + g + 1)
            nc.vector.tensor_copy(yout[:, g // 2, 0:512], banks[g % 6]).then_inc(turn_dve, 1)

    @block.tensor
    def _(pe):
        def turn(out, in_, n=P):
            return nc.tensor.transpose(out, in_, ident[0:n, 0:n])

        def part_products(lhs_h, lhs_l, rhs_h, rhs_l, runs, first, last):
            for (lo, hi), ps in runs:
                nc.tensor.matmul(ps, lhs_h, rhs_h[:, lo:hi], start=first, stop=False)
            for (lo, hi), ps in runs:
                nc.tensor.matmul(ps, lhs_h, rhs_l[:, lo:hi], start=False, stop=False)
            for (lo, hi), ps in runs:
                ins = nc.tensor.matmul(ps, lhs_l, rhs_h[:, lo:hi], start=False, stop=last)
            return ins

        def w_part(w, slot, k, m):
            return w[:, slot, k * PAIR + m * P:k * PAIR + (m + 1) * P]

        def unit_tile(slot, m, kt, rhs_h, rhs_l, k0, runs, first, last, before=None):
            for k in range(kt):
                if before is not None:
                    before(k)
                ins = part_products(w_part(wh, slot, k, m), w_part(wl, slot, k, m), rhs_h[:, k0 + k], rhs_l[:, k0 + k],
                                    runs, first and k == 0, last and k == kt - 1)
            return ins

        def unit_in(base, s, i=0):
            pe.wait_ge(w_lo, (i * 2) + (base + s + 1))
            return (base + s) % 2

        def mod_turn(q0, i=0):
            pe.wait_ge(macc_ok, (i * 2) + (q0 + 1))
            pe.wait_ge(mred_ok, (i * 2) + q0)
            for n in range(4):
                ins = turn(psA[:, n * P:(n + 1) * P], macc[:, q0 % 2, n // 2, n % 2 * P:(n % 2 + 1) * P])
            ins.then_inc(mturn_ok, 1)

        def norm_sum(r, mods_done):
            pe.wait_ge(ssum_ok, DT * (r + 1))
            pe.wait_ge(mred_ok, mods_done)
            nc.tensor.matmul(psA[:, 0:384], ones[:], ssum[:, 0:384], start=True, stop=True)
            nc.tensor.matmul(psB[:, 0:256], ones[:], ssum[:, 384:TOK], start=True, stop=True).then_inc(ms_ok, 1)

        def h_ready(r):
            return lambda k: input_split(pe, r, k)

        def ffn(f):
            r = norm_of[f"ffn{f}"]
            for part, base, count, pair0 in ffn_parts(f):
                mods, q0 = MOD_PLAN[f][part], MOD_BASE[f, part]
                cuts = sorted({0, min(count, mods // 2), count})
                for lo, hi in zip(cuts, cuts[1:]):
                    carries = 2 * lo < mods
                    if part in (0, 2):
                        if part == 2:
                            for m in range(2):
                                pe.wait_ge(res_ok[m], res_base[f, 1] + 4)

                        def pair(i):
                            t = i * 2 + (FT * f + 2 * pair0)
                            slot = unit_in(base, 0, i)
                            passed(pe, silu_ok, t)
                            unit_tile(slot, 0, DT, hh, hl, 0, runs_of(psG, 0), True, True, h_ready(r)).then_inc(gate_mm, 1)
                            unit_tile(slot, 1, DT, hh, hl, 0, runs_of(psG, 1), True, True).then_inc(gate_mm, 1)
                            if carries:
                                mod_turn(q0, i)
                            slot = unit_in(base, 1, i)
                            passed(pe, prod_ok, t)
                            unit_tile(slot, 0, DT, hh, hl, 0, runs_of(psU, 0), True, True).then_inc(up_mm, 1)
                            unit_tile(slot, 1, DT, hh, hl, 0, runs_of(psU, 1), True, True).then_inc(up_mm, 1)
                            if carries:
                                mod_turn(q0 + 1, i)
                        turns(pe, lo, hi, pair, apart=base == 0 and lo == 0)
                    else:
                        kt = HALF_TILES[part // 2] // 2
                        n_tiles = FT * f + 2 * pair_end[part]

                        def output_pair(i):
                            for s in range(2):
                                slot = unit_in(base, s, i)
                                for m in range(2):
                                    if s == 0:
                                        passed(pe, res_ok[m], i + res_base[f, part])
                                        pe.wait_ge((silu_ok, prod_ok)[m], n_tiles)
                                        pe.wait_ge(a_lo, n_tiles - kt)
                                    before = (lambda k: pe.wait_ge(a_lo, n_tiles - (kt - 1 - k))) if s == 1 and m == 0 else None
                                    ins = unit_tile(slot, m, kt, ah, al, s * kt, runs_alone((psG, psU)[m]),
                                                    s == 0, s == 1, before)
                                    if s == 1:
                                        ins.then_inc(down_mm[m], 1)
                                    elif m == 1:
                                        ins.then_inc(w_used, 1)
                                if carries:
                                    mod_turn(q0 + s, i)
                        turns(pe, lo, hi, output_pair, apart=res_base[f, part] == 0 and lo == 0)

        pe.wait_ge(const_ok, 4)
        pe.wait_ge(start_in, 16 * (len(ROWS) + 3))
        turn(psA[:, 0:N_ROWS], rows[0:N_ROWS, :], N_ROWS).then_inc(turn_mm, 1)
        turn(psB[:, 0:P], brows[:, 0, :]).then_inc(turn_mm, 1)
        turn(psB[:, P:MOD_ROWS], brows[0:MOD_ROWS - P, 1, :], MOD_ROWS - P).then_inc(turn_mm, 1)
        pe.wait_ge(x_in, 32)
        for g in range(10):
            j, half = g // 2, g % 2
            if g >= 6:
                if g % 2:
                    pe.wait_ge(turn_act, (g - 6) // 2 + 1)
                else:
                    pe.wait_ge(turn_dve, 3 + (g - 6) // 2 + 1)
            for k in range(4):
                ins = turn(banks[g % 6][:, k * P:(k + 1) * P], xin[:, j, (4 * half + k) * P:(4 * half + k + 1) * P])
            ins.then_inc(turn_mm, 1)
        pe.wait_ge(cs_ok, 2)
        pe.wait_ge(turn_dve, 3 + 5)
        pe.wait_ge(turn_act, 5)
        for b, w in enumerate((mshift, mscale)):
            pe.wait_ge(head_in[b], 16)
            for half in range(2):
                for k in range(DT):
                    ins = nc.tensor.matmul((psG, psU)[b][0:2, half, :], cs[:, k], w[:, k, half * 512:(half + 1) * 512],
                                           start=k == 0, stop=k == DT - 1)
            ins.then_inc(head_mm, 1)
        for b in range(2):
            pe.wait_ge(mrow_ok, b + 1)
            for t in range(DT):
                at = DT * b + t
                ins = turn(psA[:, 2 * at:2 * at + 2], mrow[:, at * P:(at + 1) * P], 2)
        ins.then_inc(mturn_ok, MOD_HEAD)
        mods_done = MOD_HEAD
        for name in phases:
            norm_sum(norm_of[name], mods_done)
            if name.startswith("ffn"):
                ffn(int(name[3]))
                mods_done += sum(MOD_PLAN[int(name[3])])
            elif name == "even":
                even_pe(pe, part_products, unit_tile, norm_sum)
            else:
                odd_pe(pe, part_products, unit_tile, norm_sum)
        norm_sum(norm_of["final"], mods_done)
        for g in range(10):
            j, half = g // 2, g % 2
            if j == 0:
                pe.wait_ge(hf_ok, DT * norm_of["final"] + 4 * (half + 1))
            if g >= 6:
                if g % 2:
                    pe.wait_ge(turn_act, 5 + (g - 6) // 2 + 1)
                else:
                    pe.wait_ge(turn_dve, 8 + (g - 6) // 2 + 1)
            for k in range(4):
                ins = turn(banks[g % 6][:, k * P:(k + 1) * P], x[:, 4 * half + k, j * P:(j + 1) * P])
            ins.then_inc(turn_mm, 1)


_INS = ['x_prompt', 'x_sample', 'cache_mla_ckv', 'cache_mla_krope', 'cache_diff_k', 'cache_diff_v', 'state_gla',
        'state_ret', 'c', 'c_ctx', 'mod_w', 'mod_b', 'norm_g', 'ffn_w_gate', 'ffn_w_up', 'ffn_w_down', 'even_w_in',
        'mla_q_norm', 'mla_w_uq', 'mla_kv_norm', 'mla_w_ukv', 'diff_lambda', 'diff_subln', 'even_w_out', 'odd_w_in',
        'gla_w_gate', 'gla_b_gate', 'gla_norm', 'ret_decay', 'ret_norm', 'odd_w_out', 'final_g']
_OUTS = [('y_prompt', (1, 128, 1024)), ('y_sample', (1, 512, 1024)), ('new_mla_ckv', (1, 1, 128, 256)),
         ('new_mla_krope', (1, 1, 128, 32)), ('new_diff_k', (1, 1, 128, 4, 128)), ('new_diff_v', (1, 1, 128, 4, 128)),
         ('new_state_gla', (1, 1, 2, 4, 64, 128)), ('new_state_ret', (1, 1, 2, 4, 64, 128))]


def _rope_constants():
    row = np.repeat(np.arange(T_LAT // GRID_W), GRID_W)
    col = np.tile(np.arange(GRID_W), T_LAT // GRID_W)

    def angles(pos, n):
        inv = ROPE_BASE ** (-np.arange(n // 2) * 2.0 / n)
        one = pos[:, None] * inv[None, :]
        return np.concatenate([one, one], axis=1)

    def halves(n):
        r = np.zeros((n, n))
        for i in range(n // 2):
            r[i + n // 2, i] = -1.0
            r[i, i + n // 2] = 1.0
        return r

    def both(n):
        return np.concatenate([angles(row, n // 2), angles(col, n // 2)], axis=1)

    def diagonal(block):
        n = block.shape[0]
        out = np.zeros((P, P))
        for i in range(0, P, n):
            out[i:i + n, i:i + n] = block
        return out

    tabs, rots = [], []
    for ang, block in ((both(ROPE_A), diagonal(halves(ROPE_A // 2))), (both(DH_B), diagonal(halves(DH_B // 2))),
                       (angles(np.arange(T_LAT), DK_D), diagonal(halves(DK_D)))):
        wide = np.tile(ang, (1, P // ang.shape[1])).T
        tabs.append(np.stack([np.cos(wide), np.sin(wide)], axis=1))
        rots.append(block)
    return np.stack(tabs).astype(np.float32), np.stack(rots, axis=1).astype(np.float32)


def _chunk_constants():
    s, t = np.arange(CHUNK)[:, None], np.arange(CHUNK)[None, :]
    along = np.broadcast_to(t, (P, CHUNK))
    tables = np.stack([s <= t, s >= t, along + 1, CHUNK - along, np.maximum(t - s, 0), np.maximum(s - t, 0)], axis=1)
    restart = np.ones((1, TOK))
    restart[:, ::CHUNK] = 0.0
    return tables.astype(np.float32), restart.astype(np.float32)


def kernel(**inputs):
    import concourse.bacc as _bacc
    from concourse.bass_utils import run_bass_kernel_spmd as _run

    nc = _bacc.Bacc("TRN2", target_bir_lowering=False, num_devices=1)
    arrays, args = {}, {}
    tabs, rots = _rope_constants()
    tables, restart = _chunk_constants()
    constants = [("rope_tables", tabs), ("rope_rotations", rots), ("odd_constants", tables), ("chunk_restart", restart)]
    for name, array in [(n, inputs[n]) for n in _INS] + constants:
        v = np.ascontiguousarray(array)
        arrays[f"in_{name}"] = v
        args[name] = nc.dram_tensor(f"in_{name}", v.shape, F32, kind="ExternalInput").ap()
    for name, shape in _OUTS:
        args[name] = nc.dram_tensor(f"out_{name}", shape, F32, kind="ExternalOutput").ap()
    build(nc, args)
    r = _run(nc, [arrays], core_ids=[0])
    return tuple(r.results[0][f"out_{name}"] for name, _ in _OUTS)
```
